# Optimizing a Trainium2 kernel written in Bass

```python
import jax, jax.numpy as jnp
from jax import lax
import numpy as np

D_MODEL = 1024
BATCH = 1
SEQ = 512
DEPTH = 2
DEC_BATCH = 1
DEC_SEQ = 32
PAST_LEN = 512

CHUNK = 64
Q_BLOCK = 128
N_A = DEPTH // 2
N_B = DEPTH - N_A
A_HEADS = 16
A_NOPE = 64
A_ROPE = 32
A_DQK = A_NOPE + A_ROPE
A_V = 64
Q_RANK = 384
KV_RANK = 256
ROPE_THETA = 10000.0
B_HEADS = 16
B_HD = 64
D_FF = 2816
EPS = 1e-6

kernel_name = 'yoco_mla_fox_macaron_stream_step'

def _rms_norm(x, g):
    xf = x.astype(jnp.float32)
    y = xf * lax.rsqrt(jnp.mean(xf * xf, axis=-1, keepdims=True) + EPS)
    return (y * g.astype(jnp.float32)).astype(x.dtype)

def _rope(x, pos):
    half = x.shape[-1] // 2
    inv = ROPE_THETA ** (-jnp.arange(half, dtype=jnp.float32) / half)
    ang = pos.astype(jnp.float32)[:, None] * inv[None, :]
    ang = ang.reshape((1, pos.shape[0]) + (1,) * (x.ndim - 3) + (half,))
    cos, sin = jnp.cos(ang), jnp.sin(ang)
    xf = x.astype(jnp.float32)
    x1, x2 = xf[..., :half], xf[..., half:]
    return jnp.concatenate([x1 * cos - x2 * sin, x1 * sin + x2 * cos], axis=-1).astype(x.dtype)

def _swiglu(x, w_in, w_out):
    gate, up = jnp.split(x @ w_in, 2, axis=-1)
    return (jax.nn.silu(gate) * up) @ w_out

def _attend(q, k, v, q_pos, k_pos, chunk_causal, c_q=None, c_k=None):
    s = jnp.einsum('bqhd,bkhd->bhqk', q, k, preferred_element_type=jnp.float32) * (q.shape[-1] ** -0.5)
    if c_q is not None:
        s = s + (c_q[:, :, :, None] - c_k[:, :, None, :])
    if chunk_causal:
        mask = (k_pos[None, :] // CHUNK) <= (q_pos[:, None] // CHUNK)
    else:
        mask = k_pos[None, :] <= q_pos[:, None]
    s = jnp.where(mask[None, None], s, -jnp.inf)
    p = jax.nn.softmax(s, axis=-1).astype(v.dtype)
    return jnp.einsum('bhqk,bkhd->bqhd', p, v)

def _attention(q, k, v, q_pos, k_pos, chunk_causal, c_q=None, c_k=None):
    b, lq, h, d = q.shape
    if lq < Q_BLOCK or lq % Q_BLOCK:
        return _attend(q, k, v, q_pos, k_pos, chunk_causal, c_q, c_k)
    nb = lq // Q_BLOCK
    q_blk = q.reshape(b, nb, Q_BLOCK, h, d).swapaxes(0, 1)
    pos_blk = q_pos.reshape(nb, Q_BLOCK)
    if c_q is None:
        out = lax.map(lambda a: _attend(a[0], k, v, a[1], k_pos, chunk_causal), (q_blk, pos_blk))
    else:
        c_blk = c_q.reshape(b, h, nb, Q_BLOCK).transpose(2, 0, 1, 3)
        out = lax.map(lambda a: _attend(a[0], k, v, a[1], k_pos, chunk_causal, a[2], c_k),
                      (q_blk, pos_blk, c_blk))
    return out.swapaxes(0, 1).reshape(b, lq, h, v.shape[-1])

def _mla_project(hn, pos, w_in, g_q, w_qup, g_kv, g_qn):
    b, l, _ = hn.shape
    z = hn @ w_in
    c_q = z[..., :Q_RANK]
    c_kv = z[..., Q_RANK:Q_RANK + KV_RANK]
    k_pe = z[..., Q_RANK + KV_RANK:]
    q = (_rms_norm(c_q, g_q) @ w_qup).reshape(b, l, A_HEADS, A_DQK)
    q = _rms_norm(jnp.concatenate([q[..., :A_NOPE], _rope(q[..., A_NOPE:], pos)], axis=-1), g_qn)
    return q, _rms_norm(c_kv, g_kv), _rope(k_pe, pos)

def _mla_keys(latent, k_pe, w_kvup, g_kn):
    b, l, _ = latent.shape
    kv = (latent @ w_kvup).reshape(b, l, A_HEADS, A_NOPE + A_V)
    k_pe_h = jnp.broadcast_to(k_pe[:, :, None, :], (b, l, A_HEADS, A_ROPE))
    k = _rms_norm(jnp.concatenate([kv[..., :A_NOPE], k_pe_h], axis=-1), g_kn)
    return k, kv[..., A_NOPE:]

def _fox_shared(h, g_kv, w_kvf, b_f, g_kn):
    b, l, _ = h.shape
    hd = B_HEADS * B_HD
    z = _rms_norm(h, g_kv) @ w_kvf
    k = _rms_norm(z[..., :hd].reshape(b, l, B_HEADS, B_HD), g_kn)
    v = z[..., hd:2 * hd].reshape(b, l, B_HEADS, B_HD)
    log_f = jax.nn.log_sigmoid((z[..., 2 * hd:] + b_f).astype(jnp.float32))
    return k, v, log_f

def _trunk(x, pos, past, p):
    b, l, _ = x.shape
    h = x
    lat_rows, kpe_rows = [], []
    fox = None
    for layer in range(DEPTH):
        h = h + 0.5 * _swiglu(_rms_norm(h, p['g_ffn'][layer, 0]), p['w_ffn_in'][layer, 0], p['w_ffn_out'][layer, 0])
        hn = _rms_norm(h, p['g_mix'][layer])
        if layer < N_A:
            i = layer
            q, lat, kpe = _mla_project(hn, pos, p['w_a_in'][i], p['g_a_q'][i], p['w_a_qup'][i],
                                       p['g_a_kv'][i], p['g_a_qk'][i, 0])
            lat_rows.append(lat)
            kpe_rows.append(kpe)
            if past is None:
                lat_all, kpe_all, k_pos = lat, kpe, pos
            else:
                lat_all = jnp.concatenate([past['lat'][i].astype(lat.dtype), lat], axis=1)
                kpe_all = jnp.concatenate([past['kpe'][i].astype(kpe.dtype), kpe], axis=1)
                k_pos = jnp.arange(lat_all.shape[1], dtype=jnp.int32)
            k, v = _mla_keys(lat_all, kpe_all, p['w_a_kvup'][i], p['g_a_qk'][i, 1])
            o = _attention(q, k, v, pos, k_pos, True)
            h = h + o.reshape(b, l, A_HEADS * A_V) @ p['w_a_out'][i]
        else:
            j = layer - N_A
            k_new, v_new, logf_new = fox
            if past is None:
                k_all, v_all, logf_all, k_pos = k_new, v_new, logf_new, pos
            else:
                k_all = jnp.concatenate([past['k'].astype(k_new.dtype), k_new], axis=1)
                v_all = jnp.concatenate([past['v'].astype(v_new.dtype), v_new], axis=1)
                logf_all = jnp.concatenate([past['logf'].astype(jnp.float32), logf_new], axis=1)
                k_pos = jnp.arange(k_all.shape[1], dtype=jnp.int32)
            c_k = jnp.cumsum(logf_all, axis=1).transpose(0, 2, 1)
            c_q = c_k[:, :, -l:]
            q = _rms_norm((hn @ p['w_b_q'][j]).reshape(b, l, B_HEADS, B_HD), p['g_b_qn'][j])
            o = _attention(q, k_all, v_all, pos, k_pos, False, c_q, c_k)
            h = h + o.reshape(b, l, B_HEADS * B_HD) @ p['w_b_out'][j]
        h = h + 0.5 * _swiglu(_rms_norm(h, p['g_ffn'][layer, 1]), p['w_ffn_in'][layer, 1], p['w_ffn_out'][layer, 1])
        if layer == N_A - 1:
            fox = _fox_shared(h, p['g_b_kv'], p['w_b_kvf'], p['b_b_f'], p['g_b_kn'])
    y = _rms_norm(h, p['g_final'])
    return y, jnp.stack(lat_rows), jnp.stack(kpe_rows), fox[0], fox[1], fox[2]

def setup_inputs(seed: int = 0) -> dict:
    key = jax.random.key(seed)
    ks = jax.random.split(key, 32)
    nrm = lambda k, shape: jax.random.normal(k, shape, dtype=jnp.float32)
    hd = B_HEADS * B_HD
    w_kv_part = nrm(ks[17], (D_MODEL, 2 * hd)) * D_MODEL ** -0.5
    w_f_part = nrm(ks[18], (D_MODEL, B_HEADS)) * (0.1 * D_MODEL ** -0.5)
    return {
        'x_prompt': nrm(ks[0], (BATCH, SEQ, D_MODEL)),
        'x_sample': nrm(ks[1], (DEC_BATCH, DEC_SEQ, D_MODEL)),
        'cache_mla_latent': nrm(ks[2], (N_A, DEC_BATCH, PAST_LEN, KV_RANK)),
        'cache_mla_kpe': nrm(ks[3], (N_A, DEC_BATCH, PAST_LEN, A_ROPE)),
        'cache_fox_k': nrm(ks[4], (DEC_BATCH, PAST_LEN, B_HEADS, B_HD)),
        'cache_fox_v': nrm(ks[5], (DEC_BATCH, PAST_LEN, B_HEADS, B_HD)),
        'cache_fox_logf': jax.nn.log_sigmoid(3.0 + 0.5 * nrm(ks[6], (DEC_BATCH, PAST_LEN, B_HEADS))),
        'g_ffn': 1.0 + 0.05 * nrm(ks[7], (DEPTH, 2, D_MODEL)),
        'w_ffn_in': nrm(ks[8], (DEPTH, 2, D_MODEL, 2 * D_FF)) * D_MODEL ** -0.5,
        'w_ffn_out': nrm(ks[9], (DEPTH, 2, D_FF, D_MODEL)) * D_FF ** -0.5,
        'g_mix': 1.0 + 0.05 * nrm(ks[10], (DEPTH, D_MODEL)),
        'w_a_in': nrm(ks[11], (N_A, D_MODEL, Q_RANK + KV_RANK + A_ROPE)) * D_MODEL ** -0.5,
        'g_a_q': 1.0 + 0.05 * nrm(ks[12], (N_A, Q_RANK)),
        'w_a_qup': nrm(ks[13], (N_A, Q_RANK, A_HEADS * A_DQK)) * Q_RANK ** -0.5,
        'g_a_kv': 1.0 + 0.05 * nrm(ks[14], (N_A, KV_RANK)),
        'w_a_kvup': nrm(ks[15], (N_A, KV_RANK, A_HEADS * (A_NOPE + A_V))) * KV_RANK ** -0.5,
        'g_a_qk': 1.0 + 0.05 * nrm(ks[16], (N_A, 2, A_DQK)),
        'w_a_out': nrm(ks[19], (N_A, A_HEADS * A_V, D_MODEL)) * (A_HEADS * A_V) ** -0.5,
        'g_b_kv': 1.0 + 0.05 * nrm(ks[20], (D_MODEL,)),
        'w_b_kvf': jnp.concatenate([w_kv_part, w_f_part], axis=1),
        'b_b_f': 3.0 + 0.5 * nrm(ks[21], (B_HEADS,)),
        'g_b_kn': 1.0 + 0.05 * nrm(ks[22], (B_HD,)),
        'w_b_q': nrm(ks[23], (N_B, D_MODEL, hd)) * D_MODEL ** -0.5,
        'g_b_qn': 1.0 + 0.05 * nrm(ks[24], (N_B, B_HD)),
        'w_b_out': nrm(ks[25], (N_B, hd, D_MODEL)) * hd ** -0.5,
        'g_final': 1.0 + 0.05 * nrm(ks[26], (D_MODEL,)),
    }

def reference(x_prompt, x_sample, cache_mla_latent, cache_mla_kpe, cache_fox_k, cache_fox_v, cache_fox_logf,
              g_ffn, w_ffn_in, w_ffn_out, g_mix, w_a_in, g_a_q, w_a_qup, g_a_kv, w_a_kvup, g_a_qk, w_a_out,
              g_b_kv, w_b_kvf, b_b_f, g_b_kn, w_b_q, g_b_qn, w_b_out, g_final):
    p = {'g_ffn': g_ffn, 'w_ffn_in': w_ffn_in, 'w_ffn_out': w_ffn_out, 'g_mix': g_mix,
         'w_a_in': w_a_in, 'g_a_q': g_a_q, 'w_a_qup': w_a_qup, 'g_a_kv': g_a_kv, 'w_a_kvup': w_a_kvup,
         'g_a_qk': g_a_qk, 'w_a_out': w_a_out, 'g_b_kv': g_b_kv, 'w_b_kvf': w_b_kvf, 'b_b_f': b_b_f,
         'g_b_kn': g_b_kn, 'w_b_q': w_b_q, 'g_b_qn': g_b_qn, 'w_b_out': w_b_out, 'g_final': g_final}
    pos_prompt = jnp.arange(x_prompt.shape[1], dtype=jnp.int32)
    past_len = cache_fox_k.shape[1]
    pos_sample = past_len + jnp.arange(x_sample.shape[1], dtype=jnp.int32)
    past = {'lat': cache_mla_latent, 'kpe': cache_mla_kpe, 'k': cache_fox_k, 'v': cache_fox_v,
            'logf': cache_fox_logf}
    y_prompt, p_lat, p_kpe, p_k, p_v, p_logf = _trunk(x_prompt, pos_prompt, None, p)
    y_sample, s_lat, s_kpe, s_k, s_v, s_logf = _trunk(x_sample, pos_sample, past, p)
    return (y_prompt, y_sample, p_lat, p_kpe, p_k, p_v, p_logf, s_lat, s_kpe, s_k, s_v, s_logf)


_drawn_inputs = setup_inputs


def setup_inputs(seed=0):
    import zlib

    import numpy as np

    out = dict(_drawn_inputs(seed))
    spreads = {}
    factors = {'cache_fox_logf': 5.784, 'g_a_q': 8.0, 'g_a_qk': 6.168, 'g_b_qn': 5.178}
    for name, (base, spread) in spreads.items():
        noise = np.random.default_rng([zlib.crc32(name.encode()), seed]).standard_normal(out[name].shape)
        drawn = base * np.exp(spread * noise) if base else spread * noise
        out[name] = __import__('jax').numpy.asarray(drawn.astype(out[name].dtype))
    for name, factor in factors.items():
        out[name] = (out[name] * factor).astype(out[name].dtype)
    return out
```

```python
from contextlib import ExitStack

import numpy as np

import concourse.bass as bass
from concourse import mybir

F32 = mybir.dt.float32
F32R = mybir.dt.float32r
ALU = mybir.AluOpType
ACT = mybir.ActivationFunctionType
AX = mybir.AxisListType

P = 128
D_MODEL, SEQ, DEC, PAST = 1024, 512, 32, 512
T = SEQ + DEC
KC = D_MODEL // P
NT = 5
TS = [0, 128, 256, 384, T - P]
NK = 9
KEYS = SEQ + PAST + DEC
S0 = P - DEC
D_FF = 2816
HALVES = 2
FT = D_FF // P // HALVES
HEADS = 16
PAIRS = HEADS // 2
Q_RANK, KV_RANK, NOPE, ROPE, DV, CHUNK = 384, 256, 64, 32, 64, 64
DA = NOPE + ROPE
DB = 64
DBX = DB + 2
ZW = Q_RANK + KV_RANK + ROPE
QC = Q_RANK // P
LC = KV_RANK // P
EPS = 1e-6
HALF_T = T // 2
SLOT = FT * P
NEG = -1.0e30

P_OFF = [0, 128, 384, 768, 1280]
P_W = [128, 256, 384, 512, PAST + DEC]
PT_OFF = [0, 512, 896, 1152, 1280]
PT_W = [512, 384, 256, 128, NT * DEC]
TOK_BANKS = [0, 1, 4, 5, 6, 7, 2]
MISC = 3
KSTART = [0, 128, 256, 384, KEYS - P, 512, 640, 768, 896]
W_BANKS = [3, 4, 5]
ST_MS, ST_PE, ST_RS, ST_NM, ST_RI, ST_SS, ST_VAR, ST_R = 0, 32, 48, 64, 80, 96, 136, 176
ST_F = 216

G_FFN, G_MIX, G_BKV, G_FIN, G_AQ = 0, 32, 48, 56, 64


class Steps:

    def __init__(self, sem, names, base):
        self.sem, self.names, self.base = sem, names, base

    def at(self, name, i=0):
        return self.sem, self.base + i * len(self.names) + self.names.index(name) + 1



XSPLIT = {"act": ["x_hi", "sq"], "dve": ["x_lo"], "pe": ["stat"]}
UPDATE = {"dve": ["h", "x_lo"], "act": ["x_hi", "sq"], "pe": ["stat"]}
LAST = {"dve": ["h"], "act": ["sq"], "pe": ["stat"]}
HONLY = {"dve": ["h"]}
RSTD = {"act": ["sd"], "dve": ["r"]}
FFN_IN = {"dve": ["gate", "up", "hid", "hid_lo"], "act": ["silu", "hid_hi"]}
ATT = {
    "pe": [f"s0{u}" for u in range(5)]
    + sum([[f"t0{j}", f"s1{j}"] for j in range(4)], []) + ["s14", "pv0"]
    + [f"t1{j}" for j in range(4)] + ["pv1"],
    "act": [f"exp0{u}" for u in range(5)] + sum([[f"pt0{j}", f"exp1{j}"] for j in range(4)], [])
    + ["exp14"] + [f"pt1{j}" for j in range(4)] + ["o"],
    "dve": ["m00", "m01", "r00", "m02", "r01", "m03", "r02", "m04", "r03", "r04",
            "pt00", "m10", "pt01", "m11", "r10", "pt02", "m12", "r11", "pt03", "m13", "r12", "m14", "r13", "r14"]
    + [f"pt1{j}" for j in range(4)] + ["o"],
    "pool": [f"n{h}{u}" for h in range(2) for u in range(5)],
}
STAGE = {
    "pe": ["tq0", "tq1", "tp0", "tp1", "tc0", "tc1", "ts"],
    "act": ["v", "q0", "q1", "p0", "p1", "c0", "c1", "sq", "sk"],
    "dve": ["v", "q0", "q1", "p0", "p1", "c0", "c1", "sq", "sk"],
}
PROJ = {
    "pe": ["q0", "q1", "kv0", "kv1", "kv2", "kv3"],
    "act": ["k0", "k1", "k2", "k3", "k4", "sqq", "sqk"],
    "dve": ["q0", "q1", "q2", "rope_c", "rope_a", "rope_b", "rope", "v0", "v1", "v2", "v3", "v4",
            "ssq", "ssk", "ssk2", "ms", "kn"],
    "pool": ["pow", "qn", "kpe"],
}
LATENT = {
    "pe": ["rtok"] + [f"t{j}" for j in range(6)],
    "act": [f"sq{t}" for t in range(5)] + [f"sk{t}" for t in range(5)] + ["sdq", "sdk", "sqpe", "cache", "mask"]
    + [f"t{j}" for j in range(5)] + [f"u{j}" for j in range(5)],
    "dve": ["rtok"] + [f"z{c}{t}" for c in range(2) for t in range(5)]
    + ["rc", "ra", "rb", "rope", "rstd"] + [f"cq{t}" for t in range(5)] + [f"lat{t}" for t in range(5)]
    + ["sspe", "cache"] + [f"t{j}" for j in range(5)] + [f"u{j}" for j in range(5)],
}
TOKN = {
    "act": ["sq"], "dve": ["c0", "c1", "c2", "c3", "c4", "ss", "ms", "n"], "pool": ["pow", "g"]}
TOKQ = {"act": ["sq"], "dve": TOKN["dve"], "pool": ["pow"]}
TOKV = {"dve": ["c0", "c1", "c2", "c3", "c4"]}
RTOK = {"pe": ["rtok"], "dve": ["rtok"]}
FORGET = {
    "pe": ["f", "c"], "act": ["mask", "whi", "abs", "e", "ln"],
    "dve": ["wlo", "r", "b", "min", "u", "w", "z", "a", "wz", "rb", "eb", "l", "lf", "c", "negc"]}
FSTAGE = {"pool": ["q", "cq", "ck"]}
RESPLIT = {"act": ["x_hi"], "dve": ["x_lo"]}
YOUT = {"dve": ["y"]}
PRIME = 2


def build(nc, d):
    with ExitStack() as ctx:
        def sb(name, shape, dt=F32):
            return ctx.enter_context(nc.sbuf_tensor(name, shape, dt))

        def sem(name):
            return ctx.enter_context(nc.semaphore(name))

        h = sb("h", [P, KC * T])
        xa = [sb("x_hi", [P, KC * T], F32R), sb("x_lo", [P, KC * T], F32R)]
        hid = [sb("hid_hi", [P, FT * T], F32R), sb("hid_lo", [P, FT * T], F32R)]
        raw = [sb(f"raw{s}", [P, SLOT]) for s in range(2)]
        wh = [sb(f"w_hi{s}", [P, SLOT], F32R) for s in range(2)]
        wl = [sb(f"w_lo{s}", [P, SLOT], F32R) for s in range(2)]
        scr = sb("scratch", [P, 4 * T])
        scratch = [scr[:, n * T:(n + 1) * T] for n in range(4)]
        rstd = sb("rstd", [P, T])
        rtok = sb("rtok", [P, NT])
        eps = sb("eps", [P, 1])
        neghalf = sb("neghalf", [P, 40])
        gq, gk, gbq = sb("g_q", [P, 1]), sb("g_k", [P, 1]), sb("g_bq", [P, 1])
        stat = sb("stat", [P, 304])
        gc = sb("gcols", [P, 67])
        ident = sb("ident", [P, P])
        ones = sb("ones", [P, P])
        identr = sb("identr", [P, P], F32R)
        qT = [sb("qT_hi", [P, 2 * T], F32R), sb("qT_lo", [P, 2 * T], F32R)]
        nq, nk, nv = NT * 2 * DA, NK * 2 * DA, NK * 2 * DV
        arena = sb("arena", [P, nq + nk + nv + P_OFF[4] + P_W[4]])
        qs, ks, vr = arena[:, 0:nq], arena[:, nq:nq + nk], arena[:, nq + nk:nq + nk + nv]
        prob = arena[:, nq + nk + nv:]

        start = (nc.sbuf_base + 63) // 64 * 64
        at_ = [start]

        def place(name, shape, dt=F32):
            t = nc.alloc_sbuf_tensor_at(name, shape, dt, offset=at_[0])
            n = 4
            for s in shape[1:]:
                n *= s
            at_[0] += (n + 63) // 64 * 64
            return t

        cqT = [place("cqT_hi", [P, QC * T], F32R), place("cqT_lo", [P, QC * T], F32R)]
        latT = [place("latT_hi", [P, LC * KEYS], F32R), place("latT_lo", [P, LC * KEYS], F32R)]
        kpe = place("kpe", [P, NK, ROPE])
        sspe = place("sspe", [P, NK])
        cos_sin = place("cos_sin", [P, 2, NT, ROPE])
        mask_chunk = place("mask_chunk", [P, P], F32R)
        at_[0] = start
        qn = place("q_normed", [P, NT, HEADS, DB])
        lf = place("log_forget", [P, NK, HEADS])
        cs = place("forget_sum", [P, NK, HEADS])
        ncs = place("forget_sum_neg", [P, NK, HEADS])
        gkn = place("g_kn", [P, DB])
        bf = place("b_f", [P, HEADS])
        wf = place("w_f", [P, KC * HEADS])
        wfs = [place("w_f_hi", [P, KC * HEADS], F32R), place("w_f_lo", [P, KC * HEADS], F32R)]
        tri = place("tri", [P, P])
        mask_raw = place("mask_raw", [P, P])
        mask_causal = place("mask_causal", [P, P], F32R)
        at_[0] = start
        chunk = [place(f"kv_chunk{n}", [P, NT, 512]) for n in range(2)]
        kT = [t[:, 0:2 * KEYS] for t in xa]
        vT = [t[:, 2 * KEYS:2 * KEYS + NK * 192].rearrange("p (t w) -> p t w", t=NK) for t in xa]
        pT = [t[:, KC * T:KC * T + PT_OFF[4] + PT_W[4]] for t in hid]
        lat = arena[:, 0:NT * ZW].rearrange("p (t w) -> p t w", t=NT)
        o = NT * ZW
        cached_raw, gkv, mask_tmp = arena[:, o:o + LC * PAST], arena[:, o + LC * PAST:o + LC * PAST + KV_RANK], \
            arena[:, o + LC * PAST + KV_RANK:o + LC * PAST + KV_RANK + P]

        ps = ctx.enter_context(nc.psum_tensor("ps", [P, 8, 512], F32))

        def pair(b):
            return ps[:, 2 * b:2 * b + 2, 0:HALF_T]

        def two(ap):
            return ap.rearrange("p (b n) -> p b n", b=2)

        def tile(t, k):
            return t[:, bass.ds(k * T, T)]

        def flat2(b, p0=0):
            return ps[p0:P, b:b + 2, :].rearrange("p b n -> p (b n)")[:, 0:T]

        w_load = [sem(f"w_load{s}") for s in range(2)]
        w_hi, w_lo, w_used = sem("w_hi"), sem("w_lo"), sem("w_used")
        loaded = {n: sem(f"loaded_{n}") for n in ("x", "const", "mla", "fox")}
        kv_loaded, stored = sem("kv_loaded"), sem("stored")
        stored_lf = sem("stored_log_forget")
        stored_kv = [sem("stored_kv0"), sem("stored_kv1")]
        set_dve, set_act, set_pool = sem("setup_dve"), sem("setup_act"), sem("setup_pool")
        vpad = sem("v_padding")
        kinds = dict(xsplit=XSPLIT, update=UPDATE, last=LAST, honly=HONLY, rms=RSTD, ffn=FFN_IN, att=ATT,
                     stage=STAGE, proj=PROJ, latent=LATENT, tokn=TOKN, tokq=TOKQ, tokv=TOKV, rtok=RTOK,
                     forget=FORGET, fstage=FSTAGE, resplit=RESPLIT, yout=YOUT)
        sems = {(k, e): sem(f"{k}_{e}") for k, v in kinds.items() for e in v}
        nxt = {(k, e): PRIME * len(kinds[k][e]) for k, e in sems}

        def run(kind, n=1):
            out = {}
            for e, names in kinds[kind].items():
                out[e] = Steps(sems[kind, e], names, nxt[kind, e])
                nxt[kind, e] += n * len(names)
            return out

        def prime(eng, name):
            for (k, e), s in sems.items():
                if e == name:
                    eng.sem_inc(s, PRIME * len(kinds[k][e]))

        unit = [0]
        size = {}

        def units(n, *sizes):
            for u in range(n):
                size[unit[0] + u] = sizes[u % len(sizes)]
            unit[0] += n
            return unit[0] - n

        def ffn(f, gain):
            parts = []
            for hf in range(HALVES):
                kind = "honly" if hf == 0 else "last" if gain is None else "update"
                parts.append(dict(kind="in", u=units(2 * FT, KC * P), st=run("ffn", FT), f=f, half=hf,
                                  x=None, rms=None))
                parts.append(dict(kind="out", what=kind, u=units(KC, FT * P), kt=FT, scale=0.5,
                                  st=run(kind, KC), src=("ffn", f, hf), gain=gain, first=None))
            return parts

        X0 = run("xsplit", KC)
        F0 = ffn(0, G_MIX)
        F0[0].update(x=X0, rms=run("rms"))
        Z = dict(u=units(4, 4 * ZW // 2), x=F0[3]["st"], rms=run("rms"), st=run("latent"))
        M = dict(u=units(2 * PAIRS, QC * 2 * DA, LC * 4 * DV), d=DA, proj=run("proj", PAIRS),
                 stage=run("stage", PAIRS), att=run("att", PAIRS))
        MO = dict(kind="out", what="update", u=units(KC, KC * P), kt=KC, scale=1.0, st=run("update", KC),
                  src=("a",), gain=G_FFN + 8, first=M)
        F1 = ffn(1, G_BKV)
        F1[0].update(x=MO["st"], rms=run("rms"))
        KV = dict(u=units(16, 2 * 512), x=F1[3]["st"], rms=run("rms"), rtok=run("rtok"),
                  k=[run("tokn"), run("tokn")], v=[run("tokv"), run("tokv")], forget=run("forget"),
                  resplit=run("resplit", KC))
        F2 = ffn(2, G_MIX + 8)
        F2[0].update(x=KV["resplit"])
        Q = dict(u=units(8, 2 * 512), x=F2[3]["st"], rms=run("rms"), rtok=run("rtok"),
                 k=[run("tokq"), run("tokq")])
        X = dict(d=DBX, stage=run("stage", PAIRS), att=run("att", PAIRS), fstage=run("fstage", PAIRS))
        XO = dict(kind="out", what="update", u=units(KC, KC * P), kt=KC, scale=1.0, st=run("update", KC),
                  src=("b",), gain=G_FFN + 24, first=X)
        F3 = ffn(3, None)
        F3[0].update(x=XO["st"], rms=run("rms"))
        Y = dict(x=F3[3]["st"], rms=run("rms"), yout=run("yout", KC))
        xf = [arena[:, k * T:(k + 1) * T] for k in range(KC)]
        block = ctx.enter_context(nc.Block())

        def w_uses(L, p, with_att, with_prep, mla):
            out = []
            prep = []
            if mla:
                prep = [[(f"q{n}", [("proj", "dve", f"q{n}")]) for n in range(3)],
                        [(f"kv{n}", [("proj", "dve", f"v{n}")]) for n in range(5)]]
            else:
                prep = [[], []]
            t = [[(f"t{hh}{j}", [("att", "dve", f"pt{hh}{j}")]) for j in range(4)] for hh in range(2)]
            st = [(n, [("stage", "dve", s)]) for n, s in (("tq0", "q0"), ("tq1", "q1"), ("tp0", "p0"),
                                                           ("tp1", "p1"), ("tc0", "c0"), ("tc1", "c1"), ("ts", "sk"))]
            n = 0
            for group, is_att in ((prep[0], False), (t[0], True), (prep[1], False), (t[1], True), (st, False)):
                for name, readers in group:
                    if (is_att and with_att) or (not is_att and with_prep):
                        out.append((name, W_BANKS[n % 3], p if is_att else p + 1, readers))
                    n += 1
            return out

        @block.sync
        def _(sp):
            def load(par, u, src, n):
                sp.wait_ge(w_lo, u + 1)
                sp.dma_start(raw[par][:, 0:n], src).then_inc(w_load[par], 16)

            def load_two(q, i):
                for j in range(2):
                    if q["src"][0] == "ffn":
                        src = d["w_ffn_out"][q["src"][1], q["src"][2], 2 * i + j]
                    else:
                        src = d["w_a_out" if q["src"][0] == "a" else "w_b_out"][2 * i + j]
                    load(j, q["u"] + 2 * i + j, src, q["kt"] * P)

            def load_out(q, first=0):
                with sp.Fori(first, KC // 2) as i:
                    load_two(q, i)

            def load_ffn(fs):
                for q in fs:
                    if q["kind"] == "in":
                        with sp.Fori(0, FT) as i:
                            for j in range(2):
                                load(j, q["u"] + 2 * i + j, d["w_ffn_in"][q["f"], q["half"], i, j], KC * P)
                    else:
                        load_out(q)

            n = KC * T // 2
            for k in range(2):
                sp.dma_start(h[:, k * n:(k + 1) * n], d["x"][:, k * n:(k + 1) * n]).then_inc(loaded["x"], 16)
            for dst, src in ((gc[:, :], d["g_cols"]), (ident[:, :], d["c_ident"]),
                             (gq[0:DA, :], d["g_a_qk"][0]), (gk[0:DA, :], d["g_a_qk"][1]),
                             (gbq[0:DB, :], d["g_b_qn"])):
                sp.dma_start(dst, src).then_inc(loaded["const"], 16)
            load_ffn(F0)
            for dst, src in ((cos_sin[:, :, :, :], d["c_rope"]), (kpe[:, NT:NK, :], d["kpe"]),
                             (cached_raw, d["lat_T"]), (gkv, d["g_a_kv"].to_broadcast([P, KV_RANK])),
                             (mask_tmp, d["c_mask_chunk"])):
                sp.dma_start(dst, src).then_inc(loaded["mla"], 16)
            for c in range(2):
                for k in range(2):
                    load(k, Z["u"] + 2 * c + k, d["w_a_in"][c, k], 4 * ZW // 2)
            load(0, M["u"], d["w_a_qup"][0], QC * 2 * DA)
            load(1, M["u"] + 1, d["w_a_kvup"][0], LC * 4 * DV)
            sp.wait_ge(*Z["st"]["dve"].at("lat4"))
            o_lat = d["o_lat_p"].rearrange("(t p) w -> p t w", p=P)
            sp.dma_start(o_lat, lat[:, 0:4, Q_RANK:Q_RANK + KV_RANK]).then_inc(stored, 16)
            sp.dma_start(d["o_lat_s"], lat[S0:P, 4, Q_RANK:Q_RANK + KV_RANK]).then_inc(stored, 16)
            sp.dma_start(d["o_kpe_p"].rearrange("(t p) w -> p t w", p=P), kpe[:, 0:4, :]).then_inc(stored, 16)
            sp.dma_start(d["o_kpe_s"], kpe[S0:P, 4, :]).then_inc(stored, 16)
            with sp.Fori(1, PAIRS) as i:
                load(0, M["u"] + 2 * i, d["w_a_qup"][i], QC * 2 * DA)
                load(1, M["u"] + 2 * i + 1, d["w_a_kvup"][i], LC * 4 * DV)
            load_out(MO)
            load_ffn(F1)
            sp.wait_ge(stored, 64)
            for dst, src in ((gkn[:, :], d["g_b_kn"].to_broadcast([P, DB])),
                             (bf[:, :], d["b_b_f"].to_broadcast([P, HEADS])), (mask_raw[:, :], d["c_mask_causal"]),
                             (wf[:, :], d["w_f"]), (tri[:, :], d["c_tri"]), (lf[:, NT:NK, :], d["logf"])):
                sp.dma_start(dst, src).then_inc(loaded["fox"], 16)

            for c in range(4):
                for k in range(4):
                    load(k % 2, KV["u"] + 4 * c + k, d["w_b_kv"][c, k], 2 * 512)
            load_ffn(F2)
            for c in range(2):
                for k in range(4):
                    load(k % 2, Q["u"] + 4 * c + k, d["w_b_q"][c, k], 2 * 512)
            load_two(XO, 0)
            ksx = ks[:, 0:NK * 2 * DBX].rearrange("p (t g w) -> p t g w", t=NK, g=2)
            vsx = vr.rearrange("p (t g w) -> p t g w", t=NK, g=2)
            for s in range(2):
                sp.wait_ge(stored_kv[s], 64)
            sp.wait_ge(*Q["k"][1]["dve"].at("ss"))
            with sp.Fori(0, PAIRS) as p:
                sp.wait_ge(*X["stage"]["pe"].at("ts", p - 1))
                sp.wait_ge(*X["stage"]["dve"].at("v", p - 1))
                for new_p, new_s, old, dst in (("o_k_p", "o_k_s", "fox_k", ksx), ("o_v_p", "o_v_s", "fox_v", vsx)):
                    for g in range(2):
                        cols = bass.ds(p * 2 * DB + g * DB, DB)
                        sp.dma_start(dst[:, 0:4, g, 0:DB], d[new_p].rearrange("(t p) e -> p t e", p=P)[:, :, cols]
                                     ).then_inc(kv_loaded, 16)
                        sp.dma_start(dst[S0:P, 4, g, 0:DB], d[new_s][:, cols]).then_inc(kv_loaded, 16)
                        sp.dma_start(dst[:, NT:NK, g, 0:DB], d[old].rearrange("(t p) e -> p t e", p=P)[:, :, cols]
                                     ).then_inc(kv_loaded, 16)
            load_out(XO, 1)
            load_ffn(F3)
            for k in range(KC):
                sp.wait_ge(*Y["yout"]["dve"].at("y", k))
                sp.dma_start(d["o_y"][k], xf[k]).then_inc(stored, 16)
            sp.wait_ge(stored, 16 * (4 + KC))
            sp.wait_ge(stored_lf, 32)
            for s in range(2):
                sp.wait_ge(stored_kv[s], 64)

        @block.tensor
        def _(pe):
            prime(pe, "pe")
            pe.sem_inc(w_used, PRIME)

            def product(out, lhs, rhs, start, stop):
                pe.matmul(out, lhs[0], rhs[0], start=start, stop=False)
                pe.matmul(out, lhs[0], rhs[1], start=False, stop=False)
                return pe.matmul(out, lhs[1], rhs[0], start=False, stop=stop)

            def unit_ready(u):
                pe.wait_ge(w_lo, u + PRIME + 1)

            def sum_squares(x, k):
                pe.wait_ge(*x["act"].at("sq", k))
                for n in range(2):
                    mm = pe.matmul(pair(1)[:, n, :], ones[:, :], scratch[k % 2][:, n * HALF_T:(n + 1) * HALF_T],
                                   start=(k == 0), stop=(k == KC - 1))
                mm.then_inc(x["pe"].sem, 1)

            def wide(bank, par, kt, xs, each):
                for k in range(kt):
                    if each is not None:
                        each(k)
                    w = [t[par][:, k * P:(k + 1) * P] for t in (wh, wl)]
                    for n in range(2):
                        cols = slice(k * T + n * HALF_T, k * T + (n + 1) * HALF_T)
                        mm = product(pair(bank)[:, n, :], w, [t[:, cols] for t in xs], k == 0, k == kt - 1)
                mm.then_inc(w_used, 1)

            def ffn_in(q):
                st = q["st"]["dve"]

                def tile_pair(i, first):
                    def each(k):
                        if q["x"] is not None:
                            if k == KC - 1 and q["rms"] is not None:
                                sum_squares(q["x"], KC - 1)
                            pe.wait_ge(*q["x"]["dve"].at("x_lo", k))

                    unit_ready(q["u"] + 2 * i)
                    pe.wait_ge(*st.at("gate", i - 1))
                    wide(0, 0, KC, xa, each if first else None)
                    unit_ready(q["u"] + 2 * i + 1)
                    pe.wait_ge(*st.at("up", i - 1))
                    if first and q["rms"] is not None:
                        pe.wait_ge(*q["rms"]["act"].at("sd"))
                    wide(1, 1, KC, xa, None)

                tile_pair(0, True)
                with pe.Fori(1, FT) as i:
                    tile_pair(i, False)

            def out_proj(q, before=None):
                st = q["st"]

                def tile_of(i, j, first):
                    dd = 2 * i + j
                    unit_ready(q["u"] + dd)
                    pe.wait_ge(*st["dve"].at("h", dd - 2))
                    each = None
                    if first and j == 0:
                        if before is not None:
                            def each(k):
                                pe.wait_ge(*before["st"]["dve"].at("hid_lo", k))
                        else:
                            pe.wait_ge(*q["first"]["att"]["dve"].at("o", PAIRS - 1))
                    wide(2 + j, j, q["kt"], hid, each)
                    if q["what"] != "honly" and not (first and j == 0):
                        pe_sum(i, j, first)

                def pe_sum(i, j, first):
                    pe.wait_ge(*st["act"].at("sq", 2 * i + j - 1))
                    for n in range(2):
                        mm = pe.matmul(pair(1)[:, n, :], ones[:, :],
                                       scratch[(j + 1) % 2][:, n * HALF_T:(n + 1) * HALF_T],
                                       start=(first and j == 1), stop=False)
                    mm.then_inc(st["pe"].sem, 1)

                for j in range(2):
                    tile_of(0, j, True)
                with pe.Fori(1, KC // 2) as i:
                    for j in range(2):
                        tile_of(i, j, False)

            def ffn_all(fs):
                for q in fs:
                    if q["kind"] == "in":
                        before = q
                        ffn_in(q)
                    else:
                        out_proj(q, before)

            def tok_unit(u, c, k0, kn, n, bank_free):
                unit_ready(u)
                for t in range(NT):
                    if k0 == 0:
                        bank_free(c, t)
                    out = ps[:, TOK_BANKS[(NT * c + t) % 7], 0:n]
                    for k in range(kn):
                        x = [a[:, (k0 + k) * T + TS[t]:(k0 + k) * T + TS[t] + P] for a in xa]
                        w = [a[u % 2][:, k * n:(k + 1) * n] for a in (wh, wl)]
                        mm = product(out, x, w, k0 + k == 0, k0 + k == KC - 1)
                mm.then_inc(w_used, 1)

            def token_rstd(rms, step):
                pe.wait_ge(*rms["dve"].at("r"))
                for t in range(NT):
                    mm = pe.matmul(ps[:, MISC, t:t + 1], rstd[0:1, TS[t]:TS[t] + P], ones[0:1, 0:1],
                                   start=True, stop=True)
                mm.then_inc(step.sem, 1)

            pe.wait_ge(set_dve, 7)
            for k in range(KC - 1):
                sum_squares(X0, k)
            ffn_all(F0)

            def z_free(c, t):
                if c == 0 and t == 0:
                    pe.wait_ge(*Z["x"]["dve"].at("h", KC - 1))
                elif NT * c + t >= 7:
                    pe.wait_ge(*Z["st"]["dve"].at(f"z0{NT * c + t - 7}"))
                elif TOK_BANKS[(NT * c + t) % 7] == 2:
                    pe.wait_ge(*Z["rms"]["act"].at("sd"))

            for c in range(2):
                for k in range(2):
                    pe.wait_ge(*Z["x"]["dve"].at("x_lo", 4 * k + 3))
                    tok_unit(Z["u"] + 2 * c + k, c, 4 * k, 4, ZW // 2, z_free)
                    if c == 0 and k == 0:
                        sum_squares(Z["x"], KC - 1)
                    if c == 0 and k == 1:
                        token_rstd(Z["rms"], Z["st"]["pe"])
            st = Z["st"]
            pe.wait_ge(*st["dve"].at("lat4"))
            for j in range(QC + LC):
                for t in range(4):
                    mm = pe.transpose(ps[:, j, t * P:(t + 1) * P], lat[:, t, j * P:(j + 1) * P], ident[:, :])
                mm.then_inc(st["pe"].sem, 1)
            for j in range(QC + LC):
                mm = pe.transpose(ps[:, 5, j * DEC:(j + 1) * DEC], lat[S0:P, 4, j * P:(j + 1) * P],
                                  ident[S0:P, S0:P])
            mm.then_inc(st["pe"].sem, 1)

            def attention(L, mla, mask):
                att, stg, D = L["att"], L["stage"], L["d"]
                prj = L.get("proj")
                qsv = qs[:, 0:NT * 2 * D].rearrange("p (t g w) -> p t g w", t=NT, g=2)
                ksv = ks[:, 0:NK * 2 * D].rearrange("p (t g w) -> p t g w", t=NK, g=2)

                def bank_of(name, uses, before):
                    n = [x[0] for x in uses].index(name)
                    b = uses[n][1]
                    past = [x for x in uses[:n] if x[1] == b] or [x for x in before if x[1] == b]
                    if past:
                        _, _, it, readers = past[-1]
                        for k, e, s in readers:
                            pe.wait_ge(*L[k][e].at(s, it))
                    return b

                def project_q(it, uses, before):
                    unit_ready(M["u"] + 2 * it)
                    for n in range(3):
                        b = bank_of(f"q{n}", uses, before)
                        for t in range(2 * n, min(2 * n + 2, NT)):
                            for k in range(QC):
                                mm = product(ps[:, b, (t % 2) * 2 * DA:(t % 2 + 1) * 2 * DA],
                                             [a[:, k * T + TS[t]:k * T + TS[t] + P] for a in cqT],
                                             [a[0][:, k * 2 * DA:(k + 1) * 2 * DA] for a in (wh, wl)],
                                             k == 0, k == QC - 1)
                        mm.then_inc(prj["pe"].sem if n < 2 else w_used, 1)

                def project_kv(it, uses, before):
                    unit_ready(M["u"] + 2 * it + 1)
                    for n in range(5):
                        b = bank_of(f"kv{n}", uses, before)
                        for t in range(2 * n, min(2 * n + 2, NK)):
                            for k in range(LC):
                                mm = product(ps[:, b, (t % 2) * 4 * DV:(t % 2 + 1) * 4 * DV],
                                             [a[:, k * KEYS + KSTART[t]:k * KEYS + KSTART[t] + P] for a in latT],
                                             [a[1][:, k * 4 * DV:(k + 1) * 4 * DV] for a in (wh, wl)],
                                             k == 0, k == LC - 1)
                        mm.then_inc(prj["pe"].sem if n < 4 else w_used, 1)

                def turn_staged(it, uses, before):
                    if mla:
                        pe.wait_ge(*prj["pool"].at("kpe", it))
                        pe.wait_ge(*prj["dve"].at("kn", it))
                    else:
                        pe.wait_ge(*L["fstage"]["pool"].at("ck", it))
                        pe.wait_ge(kv_loaded, 16 * 12 * (it + 1))
                    sem_ = stg["pe"].sem
                    for name, v, t0 in (("tq", qsv, 0), ("tp", ksv, 0), ("tc", ksv, NT)):
                        for g in range(2):
                            b = bank_of(f"{name}{g}", uses, before)
                            for t in range(4):
                                if name == "tc" and g == 1 and t == 3:
                                    b_ts = bank_of("ts", uses, before)
                                mm = pe.transpose(ps[0:D, b, t * P:(t + 1) * P], v[:, t0 + t, g, :], ident[:, :])
                            mm.then_inc(sem_, 1)
                    b = b_ts
                    for n, v in enumerate((qsv, ksv)):
                        for g in range(2):
                            o = (2 * n + g) * DEC
                            mm = pe.transpose(ps[0:D, b, o:o + DEC], v[S0:P, 4, g, :], ident[S0:P, S0:P])
                    mm.then_inc(sem_, 1)

                def scores(hh, u, p):
                    if u < 2:
                        name, it = f"exp{1 - hh}{3 + u}", (p - 1 if hh == 0 else p)
                    elif u == 2:
                        name, it = f"exp{1 - hh}4", (p - 1 if hh == 0 else p)
                    else:
                        name, it = f"exp{hh}{0 if u == 3 else 2}", p
                    pe.wait_ge(*att["act"].at(name, it))
                    q = [a[0:D, hh * T + TS[u]:hh * T + TS[u] + P] for a in qT]
                    k = [a[0:D, hh * KEYS:(hh + 1) * KEYS] for a in kT]
                    if u < 4:
                        out = ps[:, u % 3, 0:P_W[u]]
                        product(out, q, [a[:, 0:P_W[u]] for a in k], True, False)
                        mm = pe.matmul(out[:, u * P:(u + 1) * P], identr[:, :], mask[:, :], start=False, stop=True)
                    else:
                        mm = product(ps[:, 1, 0:PAST], q, [a[:, SEQ:SEQ + PAST] for a in k], True, True)
                        out = ps[:, 2, 0:DEC]
                        mm = product(out, q, [a[:, SEQ + PAST:KEYS] for a in k], True, mla)
                        if not mla:
                            mm = pe.matmul(out, identr[:, :], mask[:, S0:P], start=False, stop=True)
                    mm.then_inc(att["pe"].sem, 1)

                def turn(hh, j, p, uses, before):
                    if j == 0:
                        pe.wait_ge(*att["pool"].at(f"n{hh}4", p))
                    b = bank_of(f"t{hh}{j}", uses, before)
                    for u in range(j, 4):
                        mm = pe.transpose(ps[:, b, (u - j) * P:(u - j + 1) * P],
                                          prob[:, P_OFF[u] + j * P:P_OFF[u] + (j + 1) * P], ident[:, :])
                    if j == 3:
                        for jj in range(5):
                            o = P_OFF[4] + (jj * P if jj < 4 else P_W[4] - P)
                            mm = pe.transpose(ps[:, b, P + jj * DEC:P + (jj + 1) * DEC], prob[S0:P, o:o + P],
                                              ident[S0:P, S0:P])
                    mm.then_inc(att["pe"].sem, 1)

                def values(hh, p):
                    if hh == 0:
                        pe.wait_ge(*att["act"].at("o", p - 1))
                        pe.wait_ge(*att["dve"].at("o", p - 1))
                    pe.wait_ge(*att["dve"].at(f"pt{hh}3", p))
                    c = slice(hh * DV, hh * DV + P)
                    for j in range(4):
                        product(ps[:, 6, j * P:SEQ], [a[:, j, c] for a in vT],
                                [a[:, PT_OFF[j]:PT_OFF[j] + PT_W[j]] for a in pT], hh == 0 and j == 0,
                                hh == 1 and j == 3)
                    for jj in range(5):
                        r0, t = (0, NT + jj) if jj < 4 else (S0, 4)
                        o = PT_OFF[4] + jj * DEC
                        mm = product(ps[:, 7, 0:DEC], [a[r0:P, t, c] for a in vT], [a[r0:P, o:o + DEC] for a in pT],
                                     hh == 0 and jj == 0, hh == 1 and jj == 4)
                    mm.then_inc(att["pe"].sem, 1)

                def turn_of(p, prep):
                    uses = w_uses(L, p, True, prep, mla)
                    before = w_uses(L, p - 1, True, True, mla)
                    pe.wait_ge(*stg["dve"].at("sk", p))
                    for u in range(5):
                        scores(0, u, p)
                    if prep and mla:
                        project_q(p + 1, uses, before)
                    for j in range(4):
                        turn(0, j, p, uses, before)
                        scores(1, j, p)
                    scores(1, 4, p)
                    values(0, p)
                    if prep and mla:
                        project_kv(p + 1, uses, before)
                    for j in range(4):
                        turn(1, j, p, uses, before)
                    values(1, p)
                    if prep:
                        turn_staged(p + 1, uses, before)

                first = w_uses(L, -1, False, True, mla)
                if mla:
                    pe.wait_ge(*Z["st"]["dve"].at("u4"))
                    project_q(0, first, [])
                    project_kv(0, first, [])
                turn_staged(0, first, [])
                with pe.Fori(0, PAIRS - 1) as p:
                    turn_of(p, True)
                turn_of(PAIRS - 1, False)

            attention(M, True, mask_chunk)
            out_proj(MO)
            ffn_all(F1)

            def kv_free(c, t):
                n = NT * c + t
                if n == 0:
                    pe.wait_ge(*KV["x"]["dve"].at("h", KC - 1))
                elif n >= 7:
                    c0, t0 = divmod(n - 7, NT)
                    pe.wait_ge(*(KV["k"][c0] if c0 < 2 else KV["v"][c0 - 2])["dve"].at(f"c{t0}"))
                elif n == 6:
                    pe.wait_ge(*KV["rms"]["act"].at("sd"))

            for m in range(16):
                if m < 4:
                    pe.wait_ge(*KV["x"]["dve"].at("x_lo", 2 * m + 1))
                tok_unit(KV["u"] + m, m // 4, 2 * (m % 4), 2, 512, kv_free)
                if m == 0:
                    sum_squares(KV["x"], KC - 1)
                if m == 2:
                    token_rstd(KV["rms"], KV["rtok"]["pe"])
                if m == 3:
                    pe.wait_ge(*KV["rtok"]["dve"].at("rtok"))
                    pe.wait_ge(*KV["forget"]["dve"].at("wlo"))
                    for t in range(NT):
                        for k in range(KC):
                            x = [a[:, k * T + TS[t]:k * T + TS[t] + P] for a in xa]
                            w = [a[:, k * HEADS:(k + 1) * HEADS] for a in wfs]
                            mm = product(ps[:, MISC, 16 + t * HEADS:16 + (t + 1) * HEADS], x, w, k == 0, k == KC - 1)
                    mm.then_inc(KV["forget"]["pe"].sem, 1)
                if m == 9:
                    pe.wait_ge(*KV["forget"]["dve"].at("lf"))
                    for t in range(NK):
                        o = ps[:, MISC, 128 + t * HEADS:128 + (t + 1) * HEADS]
                        past = range(t) if t < 4 else range(NT, NK) if t == 4 else range(NT, t)
                        for n, s in enumerate(past):
                            pe.matmul(o, ones[:, :], lf[:, s, :], start=(n == 0), stop=False)
                        r0 = S0 if t == 4 else 0
                        mm = pe.matmul(o, tri[r0:P, :], lf[r0:P, t, :], start=len(past) == 0, stop=True)
                    mm.then_inc(KV["forget"]["pe"].sem, 1)
            pe.wait_ge(*KV["v"][1]["dve"].at("c4"))
            ffn_all(F2)

            def q_free(c, t):
                n = NT * c + t
                if n == 0:
                    pe.wait_ge(*Q["x"]["dve"].at("h", KC - 1))
                elif n >= 7:
                    pe.wait_ge(*Q["k"][0]["dve"].at(f"c{n - 7}"))
                elif n == 6:
                    pe.wait_ge(*Q["rms"]["act"].at("sd"))

            for m in range(8):
                if m < 4:
                    pe.wait_ge(*Q["x"]["dve"].at("x_lo", 2 * m + 1))
                tok_unit(Q["u"] + m, m // 4, 2 * (m % 4), 2, 512, q_free)
                if m == 0:
                    sum_squares(Q["x"], KC - 1)
                if m == 2:
                    token_rstd(Q["rms"], Q["rtok"]["pe"])
            pe.wait_ge(*Q["k"][1]["dve"].at("c4"))
            attention(X, False, mask_causal)
            out_proj(XO)
            ffn_all(F3)
            sum_squares(Y["x"], KC - 1)

        @block.scalar
        def _(act):
            prime(act, "act")

            def split_hi(par, u, loads, n):
                act.wait_ge(w_load[par], 16 * loads)
                act.wait_ge(w_used, u + 1)
                act.activation(wh[par][:, 0:n], raw[par][:, 0:n], ACT.Copy).then_inc(w_hi, 1)

            def ahead(u):
                if u < unit[0]:
                    split_hi(u % 2, u, u // 2 + 1, size[u])

            def root(rms, x):
                act.wait_ge(*x["pe"].at("stat", KC - 1))
                act.activation(two(scratch[2]), pair(1), ACT.Sqrt, bias=eps[:, 0:1], scale=1.0 / D_MODEL
                               ).then_inc(rms["act"].sem, 1)

            def split_x(k, dve_h, x, gain, par):
                if dve_h is not None:
                    act.wait_ge(*dve_h)
                act.wait_ge(*x["pe"].at("stat", k - 2))
                act.activation(tile(xa[0], k), tile(h, k), ACT.Copy, scale=gc[:, bass.ds(gain + k, 1)]
                               ).then_inc(x["act"].sem, 1)
                act.activation(scratch[par], tile(h, k), ACT.Square).then_inc(x["act"].sem, 1)

            def ffn_in(q):
                st, U = q["st"], q["u"]

                def turn(i, n_next, first):
                    split_hi(1, U + 2 * i + 1, U // 2 + i + 1, KC * P)
                    if first and q["rms"] is not None:
                        root(q["rms"], q["x"])
                    act.wait_ge(*st["dve"].at("gate", i))
                    act.activation(scratch[2], scratch[0], ACT.Silu).then_inc(st["act"].sem, 1)
                    split_hi(0, U + 2 * i + 2, U // 2 + i + 2, n_next)
                    act.wait_ge(*st["dve"].at("hid", i))
                    act.activation(tile(hid[0], i), scratch[3], ACT.Copy).then_inc(st["act"].sem, 1)

                turn(0, KC * P, True)
                with act.Fori(1, FT - 1) as i:
                    turn(i, KC * P, False)
                turn(FT - 1, size[U + 2 * FT], False)

            def out_proj(q):
                st, U, n = q["st"], q["u"], q["kt"] * P

                def turn(i, last):
                    for j in range(2):
                        if last and j == 1:
                            ahead(U + KC)
                        else:
                            split_hi((j + 1) % 2, U + 2 * i + j + 1, (U + j + 1) // 2 + i + 1, n)
                        if q["what"] == "update":
                            split_x(2 * i + j, st["dve"].at("h", 2 * i + j), st, q["gain"], j)
                        elif q["what"] == "last":
                            act.wait_ge(*st["dve"].at("h", 2 * i + j))
                            act.wait_ge(*st["pe"].at("stat", 2 * i + j - 2))
                            act.activation(scratch[j], tile(h, 2 * i + j), ACT.Square).then_inc(st["act"].sem, 1)

                with act.Fori(0, KC // 2 - 1) as i:
                    turn(i, False)
                turn(KC // 2 - 1, True)

            def ffn_all(fs):
                for q in fs:
                    ffn_in(q) if q["kind"] == "in" else out_proj(q)

            act.wait_ge(loaded["x"], 32)
            act.wait_ge(loaded["const"], 80)
            act.wait_ge(set_dve, 7)
            act.activation(identr[:, :], ident[:, :], ACT.Copy).then_inc(set_act, 1)
            ahead(0)
            for k in range(KC):
                split_x(k, None, X0, G_FFN, k % 2)
            ffn_all(F0)

            for m in range(4):
                ahead(Z["u"] + m + 1)
                if m == 0:
                    root(Z["rms"], Z["x"])
            st = Z["st"]
            inc = st["act"].sem
            act.wait_ge(*st["dve"].at("z14"))
            for o, w, col, name in ((0, Q_RANK, ST_MS, "sq"), (Q_RANK, KV_RANK, ST_MS + 5, "sk")):
                for t in range(NT):
                    if (name, t) != ("sq", 0):
                        act.wait_ge(*st["act"].at(f"{name}{t - 1}" if t else "sq4"))
                    act.activation(scratch[0][:, 0:w], lat[:, t, o:o + w], ACT.Square,
                                   accum_out=stat[:, col + t:col + t + 1]).then_inc(inc, 1)
            act.wait_ge(*st["act"].at("sk4"))
            act.activation(stat[:, ST_MS + 10:ST_MS + 15], stat[:, ST_MS:ST_MS + 5], ACT.Sqrt, bias=eps[:, 0:1],
                           scale=1.0 / Q_RANK).then_inc(inc, 1)
            act.activation(stat[:, ST_MS + 15:ST_MS + 20], stat[:, ST_MS + 5:ST_MS + 10], ACT.Sqrt,
                           bias=eps[:, 0:1], scale=1.0 / KV_RANK).then_inc(inc, 1)
            act.wait_ge(loaded["mla"], 80)
            act.wait_ge(*st["dve"].at("rope"))
            act.activation(scratch[3][:, 0:NK * ROPE], kpe[:, :, :].rearrange("p t w -> p (t w)"), ACT.Square
                           ).then_inc(inc, 1)
            new = latT[0][:, :].rearrange("p (j w) -> p j w", j=LC)
            act.activation(new[:, :, SEQ:SEQ + PAST], cached_raw.rearrange("p (j w) -> p j w", j=LC), ACT.Copy
                           ).then_inc(inc, 1)
            act.activation(mask_chunk[:, :], mask_tmp, ACT.Copy).then_inc(inc, 1)
            for j in range(QC + LC):
                act.wait_ge(*st["pe"].at(f"t{j}"))
                if j < QC:
                    act.activation(cqT[0][:, j * T:j * T + SEQ], ps[:, j, :], ACT.Copy,
                                   scale=gc[:, G_AQ + j:G_AQ + j + 1]).then_inc(inc, 1)
                else:
                    act.activation(latT[0][:, (j - QC) * KEYS:(j - QC) * KEYS + SEQ], ps[:, j, :], ACT.Copy
                                   ).then_inc(inc, 1)
            act.wait_ge(*st["pe"].at("t5"))
            for j in range(QC + LC):
                src = ps[:, 5, j * DEC:(j + 1) * DEC]
                if j < QC:
                    act.activation(cqT[0][:, j * T + SEQ:(j + 1) * T], src, ACT.Copy,
                                   scale=gc[:, G_AQ + j:G_AQ + j + 1]).then_inc(inc, 1)
                else:
                    act.activation(latT[0][:, (j - QC) * KEYS + SEQ + PAST:(j - QC + 1) * KEYS], src, ACT.Copy
                                   ).then_inc(inc, 1)

            def attention(L, mla, g_q, g_k):
                att, stg, D, U = L["att"], L["stage"], L["d"], L.get("u")
                prj = L.get("proj")
                banks = {n: b for n, b, _, _ in w_uses(L, 0, True, True, mla)}

                def exp(hh, u, p):
                    r0 = S0 if u == 4 else 0
                    c = 5 * hh + u
                    src = flat2(1, S0) if u == 4 else ps[:, u % 3, 0:P_W[u]]
                    act.wait_ge(*att["dve"].at(f"m{hh}{u}", p))
                    act.wait_ge(*att["pe"].at(f"t{1 - hh}{min(u, 3)}", p - 1 if hh == 0 else p))
                    act.activation(prob[r0:P, P_OFF[u]:P_OFF[u] + P_W[u]], src, ACT.Exp,
                                   bias=stat[r0:P, ST_NM + c:ST_NM + c + 1],
                                   accum_out=stat[r0:P, ST_RS + c:ST_RS + c + 1]).then_inc(att["act"].sem, 1)

                def split_p(hh, j, p):
                    w = PT_W[j] if j < 3 else PT_W[3] + PT_W[4]
                    act.wait_ge(*att["pe"].at(f"t{hh}{j}", p))
                    if j == 0:
                        act.wait_ge(*att["pe"].at(f"pv{1 - hh}", p - 1 if hh == 0 else p))
                    act.activation(pT[0][:, PT_OFF[j]:PT_OFF[j] + w], ps[:, banks[f"t{hh}{j}"], 0:w], ACT.Copy
                                   ).then_inc(att["act"].sem, 1)

                def project(it):
                    inc = prj["act"].sem
                    for n in range(5):
                        if n < 4:
                            act.wait_ge(*prj["pe"].at(f"kv{n}", it))
                        else:
                            act.wait_ge(w_used, U + 2 * it + 1 + PRIME + 1)
                        if n == 0:
                            act.wait_ge(*stg["pe"].at("ts", it - 1))
                        w = 2 if n < 4 else 1
                        src = ps[:, banks[f"kv{n}"], 0:w * 4 * DV].rearrange("p (t x) -> p t x", t=w)
                        dst = ks.rearrange("p (t g w) -> p t g w", t=NK, g=2)
                        act.activation(dst[:, 2 * n:2 * n + w, :, 0:NOPE],
                                       src[:, :, 0:2 * NOPE].rearrange("p t (g w) -> p t g w", g=2), ACT.Copy
                                       ).then_inc(inc, 1)
                    act.wait_ge(*prj["dve"].at("rope", it))
                    act.activation(scr[:, NK * 2 * NOPE:NK * 2 * NOPE + nq], qs, ACT.Square).then_inc(inc, 1)
                    act.wait_ge(*prj["act"].at("k4", it))
                    act.activation(scr[:, 0:NK * 2 * NOPE].rearrange("p (t w) -> p t w", w=NOPE),
                                   ks.rearrange("p (t w) -> p t w", w=DA)[:, :, 0:NOPE], ACT.Square
                                   ).then_inc(inc, 1)

                def stage(it):
                    inc = stg["act"].sem
                    act.wait_ge(*att["pe"].at("pv1", it - 1))
                    if mla:
                        act.wait_ge(*prj["dve"].at("v4", it))
                    else:
                        act.wait_ge(kv_loaded, 16 * 12 * (it + 1))
                    act.wait_ge(vpad, 2 if mla else 4)
                    dst = vT[0].rearrange("p t (g w) -> p t g w", g=3)
                    act.activation(dst[:, :, 0:3:2, :], vr.rearrange("p (t g w) -> p t g w", t=NK, g=2), ACT.Copy
                                   ).then_inc(inc, 1)
                    for name, out, n, o, g in (("tq", qT, T, 0, g_q), ("tp", kT, KEYS, 0, g_k),
                                               ("tc", kT, KEYS, SEQ, g_k)):
                        for hh in range(2):
                            act.wait_ge(*stg["pe"].at(f"{name}{hh}", it))
                            kw = {} if g is None else {"scale": g[0:D, :]}
                            act.activation(out[0][0:D, hh * n + o:hh * n + o + SEQ],
                                           ps[0:D, banks[f"{name}{hh}"], :], ACT.Copy, **kw).then_inc(inc, 1)
                    act.wait_ge(*stg["pe"].at("ts", it))
                    for n, (out, g) in enumerate(((qT, g_q), (kT, g_k))):
                        w = T if n == 0 else KEYS
                        kw = {} if g is None else {"scale": g[0:D, :]}
                        act.activation(out[0][0:D, :].rearrange("p (g w) -> p g w", g=2)[:, :, w - DEC:w],
                                       ps[0:D, banks["ts"], n * 2 * DEC:(n + 1) * 2 * DEC
                                          ].rearrange("p (g w) -> p g w", g=2), ACT.Copy, **kw).then_inc(inc, 1)

                def turn_of(p, prep):
                    for u in range(5):
                        exp(0, u, p)
                    if prep and mla:
                        split_hi(1, U + 2 * p + 3, U // 2 + p + 2, LC * 4 * DV)
                    for j in range(4):
                        split_p(0, j, p)
                        exp(1, j, p)
                    exp(1, 4, p)
                    if prep and mla:
                        project(p + 1)
                    for j in range(4):
                        split_p(1, j, p)
                    if prep and mla:
                        split_hi(0, U + 2 * p + 4, U // 2 + p + 3, KC * P)
                    act.wait_ge(*att["pe"].at("pv1", p))
                    act.activation(tile(hid[0], p), flat2(6), ACT.Copy).then_inc(att["act"].sem, 1)
                    if prep:
                        stage(p + 1)

                if mla:
                    split_hi(1, U + 1, U // 2 + 1, LC * 4 * DV)
                    act.wait_ge(stored, 64)
                    project(0)
                    split_hi(0, U + 2, U // 2 + 2, KC * P)
                stage(0)
                with act.Fori(0, PAIRS - 1) as p:
                    turn_of(p, True)
                turn_of(PAIRS - 1, False)

            attention(M, True, gq, gk)
            out_proj(MO)
            ffn_all(F1)

            def square_chunk(st, src):
                act.wait_ge(*st["dve"].at("c4"))
                act.activation(arena[:, 0:NT * 512].rearrange("p (t w) -> p t w", t=NT), src, ACT.Square
                               ).then_inc(st["act"].sem, 1)

            fg = KV["forget"]
            finc = fg["act"].sem
            f = [stat[:, ST_F:ST_F + 80], scr[:, 0:80], scr[:, 80:160], scr[:, 160:240]]
            for m in range(16):
                ahead(KV["u"] + m + 1)
                if m == 0:
                    root(KV["rms"], KV["x"])
                    act.wait_ge(loaded["fox"], 96)
                    act.activation(mask_causal[:, :], mask_raw[:, :], ACT.Copy).then_inc(finc, 1)
                    act.activation(wfs[0][:, :], wf[:, :], ACT.Copy).then_inc(finc, 1)
                if m == 5:
                    square_chunk(KV["k"][0], chunk[0][:, :, :])
                if m == 7:
                    act.wait_ge(*fg["dve"].at("b"))
                    act.activation(f[1], f[0], ACT.Abs).then_inc(finc, 1)
                    act.wait_ge(*fg["act"].at("abs"))
                    act.activation(f[2], f[1], ACT.Exp, scale=-1.0).then_inc(finc, 1)
                    act.wait_ge(*fg["dve"].at("u"))
                    act.activation(f[1], f[3], ACT.Ln).then_inc(finc, 1)
                if m == 9:
                    square_chunk(KV["k"][1], chunk[1][:, :, :])
            for k in range(KC):
                act.wait_ge(w_used, KV["u"] + 12 + k // 2 + PRIME + 1)
                act.activation(tile(xa[0], k), tile(h, k), ACT.Copy, scale=gc[:, G_FFN + 16 + k:G_FFN + 17 + k]
                               ).then_inc(KV["resplit"]["act"].sem, 1)
            ffn_all(F2)

            for m in range(8):
                ahead(Q["u"] + m + 1)
                if m == 0:
                    root(Q["rms"], Q["x"])
                if m == 5:
                    square_chunk(Q["k"][0], qn[:, :, 0:8, :].rearrange("p t g w -> p t (g w)"))
            square_chunk(Q["k"][1], qn[:, :, 8:16, :].rearrange("p t g w -> p t (g w)"))
            attention(X, False, gbq, None)
            out_proj(XO)
            ffn_all(F3)
            root(Y["rms"], Y["x"])

        @block.vector
        def _(dve):
            prime(dve, "dve")
            dve.sem_inc(w_lo, PRIME)

            def split_lo(par, u, n):
                dve.wait_ge(w_hi, u + 1)
                dve.tensor_tensor(wl[par][:, 0:n], raw[par][:, 0:n], wh[par][:, 0:n].bitcast(F32), ALU.subtract
                                  ).then_inc(w_lo, 1)

            def ahead(u):
                if u < unit[0]:
                    split_lo(u % 2, u, size[u])

            def low(out, src, hi, scale, inc):
                if scale is None:
                    ins = dve.tensor_tensor(out, src, hi.bitcast(F32), ALU.subtract)
                else:
                    ins = dve.scalar_tensor_tensor(out, src, scale, hi.bitcast(F32), ALU.mult, ALU.subtract)
                ins.then_inc(inc, 1)

            def inverse(rms):
                dve.wait_ge(*rms["act"].at("sd"))
                dve.reciprocal(rstd[:, :], scratch[2]).then_inc(rms["dve"].sem, 1)

            def split_x(k, x, gain):
                dve.wait_ge(*x["act"].at("x_hi", k))
                low(tile(xa[1], k), tile(h, k), tile(xa[0], k), gc[:, bass.ds(gain + k, 1)], x["dve"].sem)

            def ffn_in(q):
                st, U = q["st"], q["u"]
                inc = st["dve"].sem

                def turn(i, n_next, first):
                    split_lo(1, U + 2 * i + 1, KC * P)
                    if first and q["rms"] is not None:
                        inverse(q["rms"])
                        dve.wait_ge(*q["rms"]["dve"].at("r"))
                    dve.wait_ge(w_used, U + 2 * i + PRIME + 1)
                    dve.tensor_tensor(two(scratch[0]), pair(0), two(rstd[:, :]), ALU.mult).then_inc(inc, 1)
                    split_lo(0, U + 2 * i + 2, n_next)
                    dve.wait_ge(w_used, U + 2 * i + 1 + PRIME + 1)
                    dve.tensor_tensor(two(scratch[1]), pair(1), two(rstd[:, :]), ALU.mult).then_inc(inc, 1)
                    dve.wait_ge(*st["act"].at("silu", i))
                    dve.wait_ge(*st["dve"].at("up", i))
                    dve.wait_ge(*st["dve"].at("hid_lo", i - 1))
                    dve.tensor_tensor(scratch[3], scratch[2], scratch[1], ALU.mult).then_inc(inc, 1)
                    dve.wait_ge(*st["act"].at("hid_hi", i))
                    low(tile(hid[1], i), scratch[3], tile(hid[0], i), None, inc)

                turn(0, KC * P, True)
                with dve.Fori(1, FT - 1) as i:
                    turn(i, KC * P, False)
                turn(FT - 1, size[U + 2 * FT], False)

            def out_proj(q):
                st, U, n = q["st"], q["u"], q["kt"] * P

                def turn(i, last):
                    for j in range(2):
                        k = 2 * i + j
                        if last and j == 1:
                            ahead(U + KC)
                        else:
                            split_lo((j + 1) % 2, U + k + 1, n)
                        dve.wait_ge(w_used, U + k + PRIME + 1)
                        dve.scalar_tensor_tensor(two(tile(h, k)), pair(2 + j), q["scale"], two(tile(h, k)),
                                                 ALU.mult, ALU.add).then_inc(st["dve"].sem, 1)
                        if q["what"] == "update":
                            split_x(k, st, q["gain"])

                with dve.Fori(0, KC // 2 - 1) as i:
                    turn(i, False)
                turn(KC // 2 - 1, True)

            def ffn_all(fs):
                for q in fs:
                    ffn_in(q) if q["kind"] == "in" else out_proj(q)

            dve.memset(ones[:, :], 1.0).then_inc(set_dve, 1)
            dve.memset(eps[:, :], EPS).then_inc(set_dve, 1)
            dve.memset(neghalf[:, :], -0.5).then_inc(set_dve, 1)
            dve.memset(gbq[DB:DB + 2, :], 1.0).then_inc(set_dve, 1)
            dve.memset(stat[:, :], 1.0).then_inc(set_dve, 1)
            dve.wait_ge(loaded["const"], 80)
            dve.tensor_scalar(gq[0:DA, :], gq[0:DA, :], float(DA) ** -0.5, None, ALU.mult).then_inc(set_dve, 1)
            dve.tensor_scalar(gbq[0:DB, :], gbq[0:DB, :], float(DB) ** -0.5, None, ALU.mult).then_inc(set_dve, 1)
            ahead(0)
            for k in range(KC):
                split_x(k, X0, G_FFN)
            ffn_all(F0)

            def rms_tok(step):
                dve.wait_ge(*step["pe"].at("rtok"))
                dve.tensor_copy(rtok[:, :], ps[:, MISC, 0:NT]).then_inc(step["dve"].sem, 1)
                dve.wait_ge(*step["dve"].at("rtok"))

            st, U = Z["st"], Z["u"]
            inc = st["dve"].sem
            for m in range(4):
                ahead(U + m + 1)
                if m == 0:
                    inverse(Z["rms"])
                if m == 1:
                    rms_tok(st)
                if m == 2:
                    for t in range(NT):
                        dve.wait_ge(w_used, U + 1 + PRIME + 1)
                        dve.tensor_scalar(lat[:, t, 0:ZW // 2], ps[:, TOK_BANKS[t], 0:ZW // 2],
                                          rtok[:, t:t + 1], None, ALU.mult).then_inc(inc, 1)
            for t in range(NT):
                dve.wait_ge(w_used, U + 3 + PRIME + 1)
                dve.tensor_scalar(lat[:, t, ZW // 2:ZW], ps[:, TOK_BANKS[(NT + t) % 7], 0:ZW // 2],
                                  rtok[:, t:t + 1], None, ALU.mult).then_inc(inc, 1)
            dve.wait_ge(*st["dve"].at("z14"))
            dve.wait_ge(loaded["mla"], 80)
            kp = lat[:, :, Q_RANK + KV_RANK:ZW]
            hf = ROPE // 2
            ra = scr[:, 2 * T:2 * T + NT * ROPE].rearrange("p (t w) -> p t w", t=NT)
            rb = scr[:, T:T + NT * ROPE].rearrange("p (t w) -> p t w", t=NT)
            dve.tensor_tensor(ra, kp, cos_sin[:, 0], ALU.mult).then_inc(inc, 1)
            dve.tensor_tensor(rb[:, :, 0:hf], kp[:, :, hf:ROPE], cos_sin[:, 1, :, 0:hf], ALU.mult).then_inc(inc, 1)
            dve.tensor_tensor(rb[:, :, hf:ROPE], kp[:, :, 0:hf], cos_sin[:, 1, :, hf:ROPE], ALU.mult
                              ).then_inc(inc, 1)
            dve.wait_ge(*st["dve"].at("rb"))
            dve.tensor_tensor(kpe[:, 0:NT, :], ra, rb, ALU.add).then_inc(inc, 1)
            dve.wait_ge(*st["act"].at("sdk"))
            dve.reciprocal(stat[:, ST_MS + 20:ST_MS + 30], stat[:, ST_MS + 10:ST_MS + 20]).then_inc(inc, 1)
            dve.wait_ge(*st["dve"].at("rstd"))
            for t in range(NT):
                dve.tensor_scalar(lat[:, t, 0:Q_RANK], lat[:, t, 0:Q_RANK],
                                  stat[:, ST_MS + 20 + t:ST_MS + 21 + t], None, ALU.mult).then_inc(inc, 1)
            for t in range(NT):
                c = lat[:, t, Q_RANK:Q_RANK + KV_RANK]
                dve.scalar_tensor_tensor(c, c, stat[:, ST_MS + 25 + t:ST_MS + 26 + t], gkv, ALU.mult, ALU.mult
                                         ).then_inc(inc, 1)
            dve.wait_ge(*st["act"].at("sqpe"))
            dve.reduce_sum(sspe[:, :], scratch[3][:, 0:NK * ROPE].rearrange("p (t w) -> p t w", t=NK), AX.X
                           ).then_inc(inc, 1)
            dve.wait_ge(*st["act"].at("cache"))
            both = [a[:, :].rearrange("p (j w) -> p j w", j=LC)[:, :, SEQ:SEQ + PAST] for a in latT]
            low(both[1], cached_raw.rearrange("p (j w) -> p j w", j=LC), both[0], None, inc)
            for name, n, src in (("t", SEQ, None), ("u", DEC, 5)):
                for j in range(QC + LC):
                    dve.wait_ge(*st["act"].at(f"{name}{j}" if src is None else "u4"))
                    s = ps[:, j, :] if src is None else ps[:, src, j * DEC:(j + 1) * DEC]
                    if j < QC:
                        o = j * T + (0 if src is None else SEQ)
                        low(cqT[1][:, o:o + n], s, cqT[0][:, o:o + n], gc[:, G_AQ + j:G_AQ + j + 1], inc)
                    else:
                        o = (j - QC) * KEYS + (0 if src is None else SEQ + PAST)
                        low(latT[1][:, o:o + n], s, latT[0][:, o:o + n], None, inc)

            def attention(L, mla, g_q, g_k):
                att, stg, D, U = L["att"], L["stage"], L["d"], L.get("u")
                prj = L.get("proj")
                ainc = att["dve"].sem
                banks = {n: b for n, b, _, _ in w_uses(L, 0, True, True, mla)}

                def top(hh, u, p):
                    r0 = S0 if u == 4 else 0
                    c = ST_NM + 5 * hh + u
                    src = flat2(1, S0) if u == 4 else ps[:, u % 3, 0:P_W[u]]
                    dve.wait_ge(*att["pe"].at(f"s{hh}{u}", p))
                    dve.tensor_reduce(stat[r0:P, c:c + 1], src, AX.X, ALU.max, negate=True).then_inc(ainc, 1)

                def inv(hh, u, p):
                    r0 = S0 if u == 4 else 0
                    c = 5 * hh + u
                    dve.wait_ge(*att["act"].at(f"exp{hh}{u}", p))
                    dve.reciprocal(stat[r0:P, ST_RI + c:ST_RI + c + 1], stat[r0:P, ST_RS + c:ST_RS + c + 1]
                                   ).then_inc(ainc, 1)

                def split_p(hh, j, p):
                    w = PT_W[j] if j < 3 else PT_W[3] + PT_W[4]
                    dve.wait_ge(*att["act"].at(f"pt{hh}{j}", p))
                    o = slice(PT_OFF[j], PT_OFF[j] + w)
                    low(pT[1][:, o], ps[:, banks[f"t{hh}{j}"], 0:w], pT[0][:, o], None, ainc)

                def take_q(it):
                    for n in range(3):
                        if n == 0:
                            dve.wait_ge(*stg["pe"].at("ts", it - 1))
                        if n < 2:
                            dve.wait_ge(*prj["pe"].at(f"q{n}", it))
                        else:
                            dve.wait_ge(w_used, U + 2 * it + PRIME + 1)
                        w = (2 if n < 2 else 1) * 2 * DA
                        dve.tensor_copy(qs[:, n * 4 * DA:n * 4 * DA + w], ps[:, banks[f"q{n}"], 0:w]
                                        ).then_inc(prj["dve"].sem, 1)

                def project(it):
                    inc = prj["dve"].sem
                    q4 = qs.rearrange("p (t g w) -> p t g w", t=NT, g=2)
                    a = scr[:, 0:NT * 2 * ROPE].rearrange("p (t g w) -> p t g w", t=NT, g=2)
                    b = scr[:, T:T + NT * 2 * ROPE].rearrange("p (t g w) -> p t g w", t=NT, g=2)

                    def table(n, lo, hi):
                        return cos_sin[:, n, :, lo:hi].unsqueeze(2).to_broadcast([P, NT, 2, hi - lo])

                    dve.wait_ge(*prj["dve"].at("q2", it))
                    dve.wait_ge(*prj["dve"].at("ssk", it - 1))
                    dve.tensor_tensor(a, q4[:, :, :, NOPE:DA], table(0, 0, ROPE), ALU.mult).then_inc(inc, 1)
                    dve.tensor_tensor(b[:, :, :, 0:hf], q4[:, :, :, NOPE + hf:DA], table(1, 0, hf), ALU.mult
                                      ).then_inc(inc, 1)
                    dve.tensor_tensor(b[:, :, :, hf:ROPE], q4[:, :, :, NOPE:NOPE + hf], table(1, hf, ROPE), ALU.mult
                                      ).then_inc(inc, 1)
                    dve.wait_ge(*prj["dve"].at("rope_b", it))
                    dve.tensor_tensor(q4[:, :, :, NOPE:DA], a, b, ALU.add).then_inc(inc, 1)
                    for n in range(5):
                        dve.wait_ge(*prj["act"].at(f"k{n}", it))
                        if n == 0:
                            dve.wait_ge(*stg["dve"].at("v", it - 1))
                        w = 2 if n < 4 else 1
                        src = ps[:, banks[f"kv{n}"], 0:w * 4 * DV].rearrange("p (t x) -> p t x", t=w)
                        dst = vr.rearrange("p (t x) -> p t x", t=NK)
                        dve.tensor_copy(dst[:, 2 * n:2 * n + w, :], src[:, :, 2 * DV:4 * DV]).then_inc(inc, 1)
                    dve.wait_ge(*prj["act"].at("sqq", it))
                    dve.reduce_sum(stat[:, ST_SS:ST_SS + 10],
                                   scr[:, NK * 2 * NOPE:NK * 2 * NOPE + nq].rearrange("p (t w) -> p t w", w=DA),
                                   AX.X).then_inc(inc, 1)
                    dve.wait_ge(*prj["act"].at("sqk", it))
                    dve.reduce_sum(stat[:, ST_SS + 10:ST_SS + 28],
                                   scr[:, 0:NK * 2 * NOPE].rearrange("p (t w) -> p t w", w=NOPE), AX.X
                                   ).then_inc(inc, 1)
                    dve.wait_ge(*prj["dve"].at("ssk", it))
                    sk = stat[:, ST_SS + 10:ST_SS + 28].rearrange("p (t g) -> p t g", g=2)
                    dve.tensor_tensor(sk, sk, sspe[:, :].unsqueeze(2).to_broadcast([P, NK, 2]), ALU.add
                                      ).then_inc(inc, 1)
                    dve.wait_ge(*prj["dve"].at("ssk2", it))
                    dve.tensor_scalar(stat[:, ST_VAR:ST_VAR + 28], stat[:, ST_SS:ST_SS + 28], 1.0 / DA, EPS,
                                      ALU.mult, ALU.add).then_inc(inc, 1)

                def norm_keys(it):
                    dve.wait_ge(*prj["pool"].at("pow", it))
                    k3 = ks.rearrange("p (t w) -> p t w", w=DA)[:, :, 0:NOPE]
                    rk = stat[:, ST_R + 10:ST_R + 28].unsqueeze(2).to_broadcast([P, 2 * NK, NOPE])
                    dve.tensor_tensor(k3, k3, rk, ALU.mult).then_inc(prj["dve"].sem, 1)

                def stage(it):
                    inc = stg["dve"].sem
                    dve.wait_ge(*stg["act"].at("v", it))
                    v = [x.rearrange("p t (g w) -> p t g w", g=3)[:, :, 0:3:2, :] for x in vT]
                    low(v[1], vr.rearrange("p (t g w) -> p t g w", t=NK, g=2), v[0], None, inc)
                    for name, step, out, n, o, g in (("tq", "q", qT, T, 0, g_q), ("tp", "p", kT, KEYS, 0, g_k),
                                                     ("tc", "c", kT, KEYS, SEQ, g_k)):
                        for hh in range(2):
                            dve.wait_ge(*stg["act"].at(f"{step}{hh}", it))
                            c = slice(hh * n + o, hh * n + o + SEQ)
                            low(out[1][0:D, c], ps[0:D, banks[f"{name}{hh}"], :], out[0][0:D, c],
                                None if g is None else g[0:D, :], inc)
                    for n, (out, g, w) in enumerate(((qT, g_q, T), (kT, g_k, KEYS))):
                        dve.wait_ge(*stg["act"].at("sk", it))
                        o = [x[0:D, :].rearrange("p (g w) -> p g w", g=2)[:, :, w - DEC:w] for x in out]
                        low(o[1], ps[0:D, banks["ts"], n * 2 * DEC:(n + 1) * 2 * DEC
                                     ].rearrange("p (g w) -> p g w", g=2), o[0],
                            None if g is None else g[0:D, :], inc)

                def turn_of(p, prep):
                    for u in range(5):
                        top(0, u, p)
                        if u:
                            inv(0, u - 1, p)
                    inv(0, 4, p)
                    if prep and mla:
                        take_q(p + 1)
                        split_lo(1, U + 2 * p + 3, LC * 4 * DV)
                    for j in range(4):
                        split_p(0, j, p)
                        top(1, j, p)
                        if j:
                            inv(1, j - 1, p)
                    top(1, 4, p)
                    inv(1, 3, p)
                    inv(1, 4, p)
                    if prep and mla:
                        project(p + 1)
                    for j in range(4):
                        split_p(1, j, p)
                    if prep and mla:
                        split_lo(0, U + 2 * p + 4, KC * P)
                    dve.wait_ge(*att["act"].at("o", p))
                    low(tile(hid[1], p), flat2(6), tile(hid[0], p), None, ainc)
                    if prep:
                        if mla:
                            norm_keys(p + 1)
                        stage(p + 1)

                if mla:
                    split_lo(1, U + 1, LC * 4 * DV)
                    dve.wait_ge(stored, 64)
                    take_q(0)
                    project(0)
                    split_lo(0, U + 2, KC * P)
                    norm_keys(0)
                stage(0)
                with dve.Fori(0, PAIRS - 1) as p:
                    turn_of(p, True)
                turn_of(PAIRS - 1, False)

            attention(M, True, gq, gk)
            out_proj(MO)
            ffn_all(F1)

            def take_chunk(st, last_unit, c, dst, free=None):
                if free is not None:
                    dve.wait_ge(*free)
                dve.wait_ge(w_used, last_unit + PRIME + 1)
                for t in range(NT):
                    dve.tensor_scalar(dst[:, t, :], ps[:, TOK_BANKS[(NT * c + t) % 7], :], rtok[:, t:t + 1], None,
                                      ALU.mult).then_inc(st["dve"].sem, 1)

            def mean_squares(st, n_w):
                inc = st["dve"].sem
                dve.wait_ge(*st["act"].at("sq"))
                dve.reduce_sum(stat[:, ST_SS:ST_SS + 40],
                               arena[:, 0:NT * 512].rearrange("p (t w) -> p t w", w=DB), AX.X).then_inc(inc, 1)
                dve.wait_ge(*st["dve"].at("ss"))
                dve.tensor_scalar(stat[:, ST_VAR:ST_VAR + 40], stat[:, ST_SS:ST_SS + 40], 1.0 / DB, EPS, ALU.mult,
                                  ALU.add).then_inc(inc, 1)

            def normalise(st, x):
                dve.wait_ge(*st["pool"].at("pow"))
                dve.tensor_tensor(x, x, stat[:, ST_R:ST_R + 40].rearrange("p (t g) -> p t g", t=NT).unsqueeze(3)
                                  .to_broadcast([P, NT, 8, DB]), ALU.mult).then_inc(st["dve"].sem, 1)

            def heads(c):
                return chunk[c][:, :, :].rearrange("p t (g w) -> p t g w", g=8)

            fg, U = KV["forget"], KV["u"]
            finc = fg["dve"].sem
            f = [stat[:, ST_F:ST_F + 80], scr[:, 0:80], scr[:, 80:160], scr[:, 160:240], scr[:, 240:320],
                 scr[:, 320:400], scr[:, 400:480]]

            def after(name, eng="dve"):
                dve.wait_ge(*fg[eng].at(name))

            for m in range(16):
                ahead(U + m + 1)
                if m == 0:
                    inverse(KV["rms"])
                    after("whi", "act")
                    low(wfs[1][:, :], wf[:, :], wfs[0][:, :], None, finc)
                if m == 2:
                    rms_tok(KV["rtok"])
                if m == 4:
                    take_chunk(KV["k"][0], U + 3, 0, chunk[0])
                    after("f", "pe")
                    f3 = f[0].rearrange("p (t w) -> p t w", t=NT)
                    dve.tensor_tensor(f3, ps[:, MISC, 16:96].rearrange("p (t w) -> p t w", t=NT),
                                      rtok[:, :].unsqueeze(2).to_broadcast([P, NT, HEADS]), ALU.mult
                                      ).then_inc(finc, 1)
                    after("r")
                    dve.tensor_tensor(f3, f3, bf[:, :].unsqueeze(1).to_broadcast([P, NT, HEADS]), ALU.add
                                      ).then_inc(finc, 1)
                if m == 5:
                    mean_squares(KV["k"][0], DB)
                if m == 6:
                    normalise(KV["k"][0], heads(0))
                if m == 7:
                    after("b")
                    dve.tensor_scalar(f[4], f[0], 0.0, None, ALU.min).then_inc(finc, 1)
                    after("e", "act")
                    dve.tensor_scalar(f[3], f[2], 1.0, None, ALU.add).then_inc(finc, 1)
                    after("u")
                    dve.tensor_scalar(f[5], f[3], -1.0, None, ALU.add).then_inc(finc, 1)
                    after("w")
                    dve.tensor_scalar(f[6], f[5], 0.0, None, ALU.is_equal).then_inc(finc, 1)
                    after("ln", "act")
                    after("z")
                    dve.tensor_tensor(f[1], f[1], f[6], ALU.add).then_inc(finc, 1)
                    dve.tensor_tensor(f[5], f[5], f[6], ALU.add).then_inc(finc, 1)
                    after("wz")
                    dve.reciprocal(f[3], f[5]).then_inc(finc, 1)
                    after("rb")
                    dve.tensor_tensor(f[2], f[2], f[3], ALU.mult).then_inc(finc, 1)
                    after("eb")
                    dve.tensor_tensor(f[1], f[1], f[2], ALU.mult).then_inc(finc, 1)
                    after("l")
                    dve.tensor_tensor(lf[:, 0:NT, :].rearrange("p t w -> p (t w)"), f[4], f[1], ALU.subtract
                                      ).then_inc(finc, 1)
                if m == 8:
                    take_chunk(KV["k"][1], U + 7, 1, chunk[1])
                if m == 9:
                    mean_squares(KV["k"][1], DB)
                if m == 10:
                    normalise(KV["k"][1], heads(1))
                    after("c", "pe")
                    o = ps[:, MISC, 128:128 + NK * HEADS].rearrange("p (t w) -> p t w", t=NK)
                    dve.tensor_copy(cs[:, :, :], o).then_inc(finc, 1)
                    dve.tensor_scalar(ncs[:, :, :], o, -1.0, None, ALU.mult).then_inc(finc, 1)
                if m == 12:
                    take_chunk(KV["v"][0], U + 11, 2, chunk[0], (stored_kv[0], 32))
            take_chunk(KV["v"][1], U + 15, 3, chunk[1], (stored_kv[1], 32))
            for k in range(KC):
                split_x(k, KV["resplit"], G_FFN + 16)
            ffn_all(F2)

            U = Q["u"]
            qv = [qn[:, :, 8 * c:8 * c + 8, :] for c in range(2)]
            for m in range(8):
                ahead(U + m + 1)
                if m == 0:
                    inverse(Q["rms"])
                if m == 2:
                    rms_tok(Q["rtok"])
                if m == 4:
                    for s in range(2):
                        dve.wait_ge(stored_kv[s], 64)
                    take_chunk(Q["k"][0], U + 3, 0, qv[0].rearrange("p t g w -> p t (g w)"))
                if m == 5:
                    mean_squares(Q["k"][0], DB)
                if m == 6:
                    normalise(Q["k"][0], qv[0])
            take_chunk(Q["k"][1], U + 7, 1, qv[1].rearrange("p t g w -> p t (g w)"))
            mean_squares(Q["k"][1], DB)
            normalise(Q["k"][1], qv[1])
            attention(X, False, gbq, None)
            out_proj(XO)
            ffn_all(F3)
            inverse(Y["rms"])
            dve.wait_ge(*Y["rms"]["dve"].at("r"))
            for k in range(KC):
                dve.scalar_tensor_tensor(xf[k], tile(h, k), gc[:, G_FIN + k:G_FIN + k + 1], rstd[:, :], ALU.mult,
                                         ALU.mult).then_inc(Y["yout"]["dve"].sem, 1)

        @block.gpsimd
        def _(pool):
            prime(pool, "pool")
            def power(st, n):
                pool.wait_ge(*st["dve"].at("ms"))
                pool.tensor_tensor(stat[:, ST_R:ST_R + n], stat[:, ST_VAR:ST_VAR + n], neghalf[:, 0:n], ALU.pow
                                   ).then_inc(st["pool"].sem, 1)

            def attention(L, mla):
                att, stg, D = L["att"], L["stage"], L["d"]
                prj = L.get("proj")
                qsv = qs[:, 0:NT * 2 * D].rearrange("p (t g w) -> p t g w", t=NT, g=2)
                ksv = ks[:, 0:NK * 2 * D].rearrange("p (t g w) -> p t g w", t=NK, g=2)

                def stage_fox(it):
                    inc = L["fstage"]["pool"].sem
                    pool.wait_ge(*stg["pe"].at("ts", it - 1))
                    qf = qn[:, :, :, :].rearrange("p t g w -> p t (g w)")
                    pool.tensor_copy(qsv[:, :, :, 0:DB], qf[:, :, bass.ds(it * 2 * DB, 2 * DB)]
                                     .rearrange("p t (g w) -> p t g w", g=2)).then_inc(inc, 1)
                    for dst, src, n in ((qsv[:, :, :, DB + 1], cs, NT), (ksv[:, :, :, DB], ncs, NK)):
                        pool.tensor_copy(dst, src[:, 0:n, bass.ds(it * 2, 2)]).then_inc(inc, 1)

                def turn_of(p, prep):
                    for hh in range(2):
                        for u in range(5):
                            r0, c = (S0 if u == 4 else 0), 5 * hh + u
                            x = prob[r0:P, P_OFF[u]:P_OFF[u] + P_W[u]]
                            if u == 4 or (hh, u) == (1, 0):
                                pool.wait_ge(*att["pool"].at(f"n{hh}{3}" if u == 4 else "n04", p))
                            pool.wait_ge(*att["dve"].at(f"r{hh}{u}", p))
                            by = stat[r0:P, ST_RI + c:ST_RI + c + 1].to_broadcast([P - r0, P_W[u]])
                            pool.tensor_tensor(x, x, by, ALU.mult).then_inc(att["pool"].sem, 1)
                    pool.wait_ge(*att["pool"].at("n14", p))
                    if prep:
                        if mla:
                            project_at(p + 1)
                        else:
                            stage_fox(p + 1)

                def project_at(it):
                    pool.wait_ge(*prj["dve"].at("ms", it))
                    pool.tensor_tensor(stat[:, ST_R:ST_R + 28], stat[:, ST_VAR:ST_VAR + 28], neghalf[:, 0:28],
                                       ALU.pow).then_inc(prj["pool"].sem, 1)
                    pool.wait_ge(*prj["pool"].at("pow", it))
                    q3 = qs.rearrange("p (t w) -> p t w", w=DA)
                    pool.tensor_tensor(q3, q3, stat[:, ST_R:ST_R + 10].unsqueeze(2).to_broadcast([P, 10, DA]),
                                       ALU.mult).then_inc(prj["pool"].sem, 1)
                    pool.tensor_tensor(ksv[:, :, :, NOPE:DA],
                                       kpe[:, :, :].unsqueeze(2).to_broadcast([P, NK, 2, ROPE]),
                                       stat[:, ST_R + 10:ST_R + 28].rearrange("p (t g) -> p t g", g=2).unsqueeze(3)
                                       .to_broadcast([P, NK, 2, ROPE]), ALU.mult).then_inc(prj["pool"].sem, 1)

                if mla:
                    project_at(0)
                else:
                    stage_fox(0)
                with pool.Fori(0, PAIRS - 1) as p:
                    turn_of(p, True)
                turn_of(PAIRS - 1, False)

            def pad():
                for a in vT:
                    pool.memset(a[:, :, DV:2 * DV].bitcast(F32), 0.0).then_inc(vpad, 1)

            pool.wait_ge(w_used, Z["u"] + 3 + PRIME + 1)
            pad()
            attention(M, True)
            def store_kv(c):
                if c < 2:
                    pool.wait_ge(*KV["k"][c]["pool"].at("g"))
                else:
                    pool.wait_ge(*KV["v"][c - 2]["dve"].at("c4"))
                o, cols = "o_k" if c < 2 else "o_v", slice((c % 2) * 512, (c % 2) * 512 + 512)
                pool.dma_start(d[o + "_p"].rearrange("(t p) e -> p t e", p=P)[:, :, cols], chunk[c % 2][:, 0:4, :]
                             ).then_inc(stored_kv[c % 2], 16)
                pool.dma_start(d[o + "_s"][:, cols], chunk[c % 2][S0:P, 4, :]).then_inc(stored_kv[c % 2], 16)

            for c in range(2):
                st = KV["k"][c]
                power(st, 40)
                pool.wait_ge(*st["dve"].at("n"))
                x = chunk[c][:, :, :].rearrange("p t (g w) -> p (t g) w", g=8)
                pool.tensor_tensor(x, x, gkn[:, :].unsqueeze(1).to_broadcast([P, 40, DB]), ALU.mult
                                   ).then_inc(st["pool"].sem, 1)
                store_kv(c)
            pool.wait_ge(*KV["forget"]["dve"].at("lf"))
            pool.dma_start(d["o_lf_p"].rearrange("(t p) w -> p t w", p=P), lf[:, 0:4, :]).then_inc(stored_lf, 16)
            pool.dma_start(d["o_lf_s"], lf[S0:P, 4, :]).then_inc(stored_lf, 16)
            for c in range(2, 4):
                store_kv(c)
            pool.wait_ge(w_used, Q["u"] + 7 + PRIME + 1)
            for c in range(2):
                power(Q["k"][c], 40)
            pad()
            qx = qs[:, 0:NT * 2 * DBX].rearrange("p (t w) -> p t w", w=DBX)
            kx = ks[:, 0:NK * 2 * DBX].rearrange("p (t w) -> p t w", w=DBX)
            pool.wait_ge(*Q["k"][1]["dve"].at("ss"))
            pool.memset(qx[:, :, DB:DB + 1], 1.0).then_inc(set_pool, 1)
            pool.memset(kx[:, :, DB + 1:DB + 2], 1.0).then_inc(set_pool, 1)
            attention(X, False)


INS = {
    "x": (P, KC * T), "g_cols": (P, 67), "g_a_qk": (2, DA, 1), "g_b_qn": (DB, 1), "g_a_kv": (1, KV_RANK),
    "g_b_kn": (1, DB), "b_b_f": (1, HEADS), "w_ffn_in": (4, HALVES, FT, 2, P, KC * P),
    "w_ffn_out": (4, HALVES, KC, P, FT * P), "w_a_in": (2, 2, P, 4 * ZW // 2), "w_a_qup": (PAIRS, P, QC * 2 * DA),
    "w_a_kvup": (PAIRS, P, LC * 4 * DV), "w_a_out": (KC, P, KC * P), "w_b_kv": (4, 4, P, 1024),
    "w_f": (P, KC * HEADS), "w_b_q": (2, 4, P, 1024), "w_b_out": (KC, P, KC * P), "kpe": (P, 4, ROPE),
    "lat_T": (P, LC * PAST), "fox_k": (PAST, D_MODEL), "fox_v": (PAST, D_MODEL), "logf": (P, 4, HEADS),
    "c_ident": (P, P), "c_mask_chunk": (P, P), "c_mask_causal": (P, P), "c_tri": (P, P),
    "c_rope": (P, 2, NT, ROPE),
}
OUTS = {
    "o_y": (KC, P, T), "o_lat_p": (SEQ, KV_RANK), "o_lat_s": (DEC, KV_RANK), "o_kpe_p": (SEQ, ROPE),
    "o_kpe_s": (DEC, ROPE), "o_k_p": (SEQ, D_MODEL), "o_k_s": (DEC, D_MODEL), "o_v_p": (SEQ, D_MODEL),
    "o_v_s": (DEC, D_MODEL), "o_lf_p": (SEQ, HEADS), "o_lf_s": (DEC, HEADS),
}


def constants():
    i = np.arange(P)
    out = {"c_ident": np.eye(P, dtype=np.float32),
           "c_tri": (i[:, None] <= i[None, :]).astype(np.float32),
           "c_mask_chunk": np.where(i[None, :] // CHUNK <= i[:, None] // CHUNK, 0.0, NEG).astype(np.float32),
           "c_mask_causal": np.where(i[None, :] <= i[:, None], 0.0, NEG).astype(np.float32)}
    half = ROPE // 2
    pos = np.concatenate([np.arange(SEQ), PAST + np.arange(DEC)]).astype(np.float32)
    inv = (np.float32(10000.0) ** (-np.arange(half, dtype=np.float32) / np.float32(half))).astype(np.float32)
    ang = (pos[:, None] * inv[None, :]).astype(np.float32).astype(np.float64)
    cos, sin = np.cos(ang), np.sin(ang)
    table = np.stack([np.concatenate([cos, cos], 1), np.concatenate([-sin, sin], 1)]).astype(np.float32)
    rope = np.stack([table[:, s:s + P] for s in TS])
    out["c_rope"] = np.ascontiguousarray(rope.transpose(2, 1, 0, 3))
    return out


def kernel(**inputs):
    import concourse.bacc as bacc
    from concourse.bass_utils import run_bass_kernel_spmd

    a = {k: np.asarray(v) for k, v in inputs.items()}

    def cols(g):
        g = g.reshape(-1, g.shape[-1])
        return g.reshape(g.shape[0], -1, P).transpose(2, 0, 1).reshape(P, -1)

    x = np.concatenate([a["x_prompt"][0], a["x_sample"][0]], 0).T
    arrays = dict(constants())
    arrays["x"] = x.reshape(KC, P, T).transpose(1, 0, 2).reshape(P, KC * T)
    arrays["g_cols"] = np.concatenate([cols(a["g_ffn"]), cols(a["g_mix"]), cols(a["g_b_kv"]), cols(a["g_final"]),
                                       cols(a["g_a_q"])], 1)
    arrays["g_a_qk"] = a["g_a_qk"].reshape(2, DA, 1)
    arrays["g_b_qn"] = a["g_b_qn"][0].reshape(DB, 1)
    arrays["g_a_kv"] = a["g_a_kv"].reshape(1, KV_RANK)
    arrays["g_b_kn"] = a["g_b_kn"].reshape(1, DB)
    arrays["b_b_f"] = a["b_b_f"].reshape(1, HEADS)
    arrays["w_ffn_in"] = a["w_ffn_in"].reshape(4, KC, P, 2, HALVES, FT, P).transpose(0, 4, 5, 3, 2, 1, 6).reshape(
        INS["w_ffn_in"])
    arrays["w_ffn_out"] = a["w_ffn_out"].reshape(4, HALVES, FT, P, KC, P).transpose(0, 1, 4, 3, 2, 5).reshape(
        INS["w_ffn_out"])
    arrays["w_a_in"] = a["w_a_in"][0].reshape(2, 4, P, 2, ZW // 2).transpose(3, 0, 2, 1, 4).reshape(INS["w_a_in"])
    arrays["w_a_qup"] = a["w_a_qup"][0].reshape(QC, P, PAIRS, 2 * DA).transpose(2, 1, 0, 3).reshape(INS["w_a_qup"])
    arrays["w_a_kvup"] = a["w_a_kvup"][0].reshape(LC, P, PAIRS, 2, 2, DV).transpose(2, 1, 0, 4, 3, 5).reshape(
        INS["w_a_kvup"])
    for n in "ab":
        arrays[f"w_{n}_out"] = a[f"w_{n}_out"][0].reshape(KC, P, KC, P).transpose(2, 1, 0, 3).reshape(
            INS["w_a_out"])
    kvf = a["w_b_kvf"]
    arrays["w_b_kv"] = kvf[:, :2 * D_MODEL].reshape(4, 2, P, 4, 512).transpose(3, 0, 2, 1, 4).reshape(INS["w_b_kv"])
    arrays["w_f"] = kvf[:, 2 * D_MODEL:].reshape(KC, P, HEADS).transpose(1, 0, 2).reshape(INS["w_f"])
    arrays["w_b_q"] = a["w_b_q"][0].reshape(4, 2, P, 2, 512).transpose(3, 0, 2, 1, 4).reshape(INS["w_b_q"])
    arrays["kpe"] = a["cache_mla_kpe"][0, 0].reshape(4, P, ROPE).transpose(1, 0, 2)
    arrays["lat_T"] = a["cache_mla_latent"][0, 0].T.reshape(LC, P, PAST).transpose(1, 0, 2).reshape(INS["lat_T"])
    arrays["fox_k"] = a["cache_fox_k"][0].reshape(PAST, D_MODEL)
    arrays["fox_v"] = a["cache_fox_v"][0].reshape(PAST, D_MODEL)
    arrays["logf"] = a["cache_fox_logf"][0].reshape(4, P, HEADS).transpose(1, 0, 2)
    arrays = {k: np.ascontiguousarray(v) for k, v in arrays.items()}

    nc = bacc.Bacc("TRN2", target_bir_lowering=False, num_devices=1)
    d = {n: nc.dram_tensor(n, s, F32, kind="ExternalInput").ap() for n, s in INS.items()}
    d |= {n: nc.dram_tensor(n, s, F32, kind="ExternalOutput").ap() for n, s in OUTS.items()}
    build(nc, d)
    r = run_bass_kernel_spmd(nc, [arrays], core_ids=[0]).results[0]
    y = r["o_y"].reshape(D_MODEL, T).T
    return (np.ascontiguousarray(y[:SEQ])[None], np.ascontiguousarray(y[SEQ:])[None],
            r["o_lat_p"][None, None], r["o_kpe_p"][None, None],
            r["o_k_p"].reshape(1, SEQ, HEADS, DB), r["o_v_p"].reshape(1, SEQ, HEADS, DB), r["o_lf_p"][None],
            r["o_lat_s"][None, None], r["o_kpe_s"][None, None],
            r["o_k_s"].reshape(1, DEC, HEADS, DB), r["o_v_s"].reshape(1, DEC, HEADS, DB), r["o_lf_s"][None])
```

```python
from contextlib import ExitStack

import numpy as np

import concourse.bass as bass
from concourse import mybir

F32 = mybir.dt.float32
F32R = mybir.dt.float32r
ALU = mybir.AluOpType
ACT = mybir.ActivationFunctionType
AX = mybir.AxisListType

P = 128
D_MODEL, SEQ, DEC, PAST = 1024, 512, 32, 512
T = SEQ + DEC
KC = D_MODEL // P
NT = 5
TS = [0, 128, 256, 384, T - P]
NK = 9
KEYS = SEQ + PAST + DEC
S0 = P - DEC
D_FF = 2816
HALVES = 2
FT = D_FF // P // HALVES
HEADS = 16
PAIRS = HEADS // 2
Q_RANK, KV_RANK, NOPE, ROPE, DV, CHUNK = 384, 256, 64, 32, 64, 64
DA = NOPE + ROPE
DB = 64
DBX = DB + 2
ZW = Q_RANK + KV_RANK + ROPE
QC = Q_RANK // P
LC = KV_RANK // P
EPS = 1e-6
X_PARTS = 4
HALF_T = T // 2
SLOT = FT * P
NEG = -1.0e30

P_OFF = [0, 128, 384, 768, 1280]
P_W = [128, 256, 384, 512, PAST + DEC]
PT_W = [512, 384, 256, 128]
PT_S = NT * DEC
PT_OFF = [0, 512, 896, 1152 + PT_S]
PS_OFF = [1152, 1280 + PT_S]
TOK_BANKS = [0, 1, 4, 5, 6, 7, 2]
F_BANKS = [7, 2]
MISC = 3
KSTART = [0, 128, 256, 384, KEYS - P, 512, 640, 768, 896]
W_BANKS = [3, 4, 5]
ST_MS, ST_RS, ST_NM, ST_RI, ST_SS, ST_VAR, ST_R = 0, 48, 64, 80, 96, 136, 176
ST_F = 216

G_FFN, G_MIX, G_BKV, G_FIN, G_AQ = 0, 32, 48, 56, 64


class Steps:

    def __init__(self, sem, names, base):
        self.sem, self.names, self.base = sem, names, base

    def at(self, name, i=0):
        return self.sem, self.base + i * len(self.names) + self.names.index(name) + 1


XSPLIT = {"act": ["x_hi", "sq"], "dve": ["x_lo"], "pe": ["stat"]}
UPDATE = {"dve": ["h", "x_lo"], "act": ["x_hi", "sq"], "pe": ["stat"]}
LAST = {"dve": ["h"], "act": ["sq"], "pe": ["stat"]}
HONLY = {"dve": ["h"]}
RSTD = {"act": ["sd"], "dve": ["r"]}
FFN_IN = {"dve": ["gate", "up", "hid", "hid_lo"], "act": ["silu", "hid_hi"]}
def skewed(first, then):
    out = [first[0]]
    for n in range(1, len(first)):
        out += [first[n], then[n - 1]]
    return out + then[len(first) - 1:]


HEAD0 = {
    "pe": [f"s0{u}" for u in range(5)], "act": [f"exp0{u}" for u in range(5)],
    "dve": [f"m0{u}" for u in range(5)] + ["r0"], "pool": [f"d0{u}" for u in range(5)]}
ATT = {
    "pe": sum([[f"t0{j}", f"s1{j}"] for j in range(4)], []) + ["s14", "pv0"] + [f"t1{j}" for j in range(4)] + ["pv1"],
    "act": skewed([f"pt0{j}" for j in range(4)], [f"exp1{u}" for u in range(5)]) + [f"pt1{j}" for j in range(4)]
    + ["o", "os0", "os1"],
    "dve": sum([[f"m1{j}", f"pt0{j}"] for j in range(4)], []) + ["m14", "r1"] + [f"pt1{j}" for j in range(4)]
    + ["op", "os0", "o"],
    "pool": [f"d1{u}" for u in range(5)],
}
STAGE = {
    "pe": ["tq0", "tq1", "tp0", "tp1", "tc0", "tc1", "ts"],
    "act": ["q0", "q1", "p0", "p1", "c0", "c1", "sq", "sk"],
    "dve": ["q0", "q1", "p0", "p1", "c0", "c1", "sq", "sk"],
}
STAGEV = {"act": ["vp", "v"], "pool": ["vp", "v"]}
PROJ = {
    "pe": ["q0", "q1", "kv0", "kv1", "kv2", "kv3"],
    "act": ["sqq", "k0", "k1", "k2", "k3", "k4", "sqk"],
    "dve": ["q0", "q1", "q2", "rope_c", "rope_a", "rope_b", "rope", "v0", "v1", "ssq", "msq", "v2", "v3", "v4",
            "ssk", "ssk2", "ms", "kn"],
    "pool": ["powq", "qn", "pow", "kpe"],
}
LATENT = {
    "pe": ["rtok"] + [f"t{j}" for j in range(6)],
    "act": [f"sq{t}" for t in range(5)] + [f"sk{t}" for t in range(5)] + ["sdq", "sdk", "sqpe", "cache", "mask"]
    + [f"t{j}" for j in range(5)] + [f"u{j}" for j in range(5)],
    "dve": ["rtok"] + [f"z{c}{t}" for c in range(2) for t in range(5)]
    + ["rc", "ra", "rb", "rope", "rstd"] + [f"cq{t}" for t in range(5)] + [f"lat{t}" for t in range(5)]
    + ["sspe", "cache"] + [f"t{j}" for j in range(5)] + [f"u{j}" for j in range(5)],
}
TOKN = {
    "act": ["sq"], "dve": ["c0", "c1", "c2", "c3", "c4", "ss", "ms", "n"], "pool": ["pow", "g"]}
TOKQ = {"act": ["sq", "sq4"], "dve": ["c0", "c1", "c2", "c3", "c4", "ss", "ss4", "ms", "n"], "pool": ["pow"]}
TOKQ1 = {"act": TOKQ["act"], "dve": TOKQ["dve"][:-1], "pool": ["pow", "n"]}
TOKV = {"dve": ["c0", "c1", "c2", "c3", "c4"]}
RTOK = {"pe": ["rtok"], "dve": ["rtok"]}
FORGET = {
    "pe": ["f", "ft", "c"], "act": ["mask", "whi", "abs", "e", "ln"],
    "dve": ["wlo", "fs0", "fs1", "b", "min", "u", "w", "z", "a", "wz", "rb", "eb", "l", "lf", "c", "negc"]}
FSTAGE = {"pool": ["q", "cq", "ck"]}
RESPLIT = {"act": ["x_hi"], "dve": ["x_lo"]}
YOUT = {"dve": ["y"]}
PRIME = 2


def build(nc, d):
    with ExitStack() as ctx:
        def sb(name, shape, dt=F32):
            return ctx.enter_context(nc.sbuf_tensor(name, shape, dt))

        def sem(name):
            return ctx.enter_context(nc.semaphore(name))

        h = sb("h", [P, KC * T])
        xa = [sb("x_hi", [P, KC * T], F32R), sb("x_lo", [P, KC * T], F32R)]
        hid = [sb("hid_hi", [P, FT * T], F32R), sb("hid_lo", [P, FT * T], F32R)]
        raw = [sb(f"raw{s}", [P, SLOT]) for s in range(2)]
        wh = [sb(f"w_hi{s}", [P, SLOT], F32R) for s in range(2)]
        wl = [sb(f"w_lo{s}", [P, SLOT], F32R) for s in range(2)]
        scr = sb("scratch", [P, 4 * T])
        scratch = [scr[:, n * T:(n + 1) * T] for n in range(4)]
        rstd = sb("rstd", [P, T])
        rtok = sb("rtok", [P, NT])
        eps = sb("eps", [P, 1])
        neghalf = sb("neghalf", [P, 40])
        gq, gk, gbq = sb("g_q", [P, 1]), sb("g_k", [P, 1]), sb("g_bq", [P, 1])
        stat = sb("stat", [P, 304])
        gc = sb("gcols", [P, 67])
        ident = sb("ident", [P, P])
        ones = sb("ones", [P, P])
        identr = sb("identr", [P, P], F32R)
        qT = [sb("qT_hi", [P, 2 * T], F32R), sb("qT_lo", [P, 2 * T], F32R)]
        nq, nk, nv = NT * 2 * DA, NK * 2 * DA, NK * 2 * DV
        arena = sb("arena", [P, nq + nk + nv + P_OFF[4] + P_W[4]])
        qs, ks, vr = arena[:, 0:nq], arena[:, nq:nq + nk], arena[:, nq + nk:nq + nk + nv]
        prob = arena[:, nq + nk + nv:]

        start = (nc.sbuf_base + 63) // 64 * 64
        at_ = [start]

        def place(name, shape, dt=F32):
            t = nc.alloc_sbuf_tensor_at(name, shape, dt, offset=at_[0])
            n = 4
            for s in shape[1:]:
                n *= s
            at_[0] += (n + 63) // 64 * 64
            return t

        cqT = [place("cqT_hi", [P, QC * T], F32R), place("cqT_lo", [P, QC * T], F32R)]
        latT = [place("latT_hi", [P, LC * KEYS], F32R), place("latT_lo", [P, LC * KEYS], F32R)]
        kpe = place("kpe", [P, NK, ROPE])
        sspe = place("sspe", [P, NK])
        cos_sin = place("cos_sin", [P, 2, NT, ROPE])
        mask_chunk = place("mask_chunk", [P, P], F32R)
        at_[0] = start
        qn = place("q_normed", [P, NT, HEADS, DB])
        lf = place("log_forget", [P, NK, HEADS])
        cs = place("forget_sum", [P, NK, HEADS])
        ncs = place("forget_sum_neg", [P, NK, HEADS])
        gkn = place("g_kn", [P, DB])
        bf = place("b_f", [P, HEADS])
        wf = place("w_f", [P, KC * HEADS])
        WF = (KC - 1) * HEADS + P
        wfs = [place("w_f_hi", [P, WF], F32R), place("w_f_lo", [P, WF], F32R)]
        fT = scr[0:HEADS, T:2 * T]
        tri = place("tri", [P, P])
        mask_raw = place("mask_raw", [P, P])
        mask_causal = place("mask_causal", [P, P], F32R)
        at_[0] = start
        chunk = [place(f"kv_chunk{n}", [P, NT, 512]) for n in range(2)]
        kT = [t[:, 0:2 * KEYS] for t in xa]
        vT = [t[:, 2 * KEYS:2 * KEYS + 4 * 192].rearrange("p (t w) -> p t w", t=4) for t in xa]
        vsT = [t[:, 2 * KEYS + 4 * 192:2 * KEYS + 4 * 192 + NT * 128].rearrange("p (t w) -> p t w", t=NT) for t in xa]
        pT = [t[:, KC * T:KC * T + PS_OFF[1] + PT_S] for t in hid]
        apart = PS_OFF[1] - PS_OFF[0]
        o = FT * T - 2 * apart
        pS = [t[:, o:].rearrange("p (g w) -> p g w", g=2)[:, :, KC * T + PS_OFF[0] - o:KC * T + PS_OFF[0] - o + PT_S]
              for t in hid]
        lat = arena[:, 0:NT * ZW].rearrange("p (t w) -> p t w", t=NT)
        o = NT * ZW
        cached_raw, gkv, mask_tmp = arena[:, o:o + LC * PAST], arena[:, o + LC * PAST:o + LC * PAST + KV_RANK], \
            arena[:, o + LC * PAST + KV_RANK:o + LC * PAST + KV_RANK + P]

        diag = [raw[u // 3][:, KC * P + u % 3 * P:KC * P + (u % 3 + 1) * P] for u in range(5)]

        ps = ctx.enter_context(nc.psum_tensor("ps", [P, 8, 512], F32))

        vrv = vr.rearrange("p (t g w) -> p t g w", t=NK, g=2)
        v_parts = ((vrv[:, 0:4], [x.rearrange("p t (g w) -> p t g w", g=3)[:, :, 0:3:2, :] for x in vT]),
                   (vrv[:, 4:NK], [x.rearrange("p t (g w) -> p t g w", g=2) for x in vsT]))

        def pair(b):
            return ps[:, 2 * b:2 * b + 2, 0:HALF_T]

        def two(ap):
            return ap.rearrange("p (b n) -> p b n", b=2)

        def tile(t, k):
            return t[:, bass.ds(k * T, T)]

        w_load = [sem(f"w_load{s}") for s in range(2)]
        w_hi, w_lo, w_used = sem("w_hi"), sem("w_lo"), sem("w_used")
        loaded = {n: sem(f"loaded_{n}") for n in ("gains", "const", "mla", "fox")}
        loaded["x"] = [sem(f"loaded_x{k}") for k in range(X_PARTS)]
        k_loaded, v_loaded, stored = sem("k_loaded"), sem("v_loaded"), sem("stored")
        stored_lf = sem("stored_log_forget")
        stored_kv = [sem("stored_kv0"), sem("stored_kv1")]
        set_dve, set_act, set_pool = sem("setup_dve"), sem("setup_act"), sem("setup_pool")
        vpad = sem("v_padding")
        kinds = dict(head0=HEAD0, stagev=STAGEV, xsplit=XSPLIT, update=UPDATE, last=LAST, honly=HONLY, rms=RSTD, ffn=FFN_IN, att=ATT,
                     stage=STAGE, proj=PROJ, latent=LATENT, tokn=TOKN, tokq=TOKQ, tokq1=TOKQ1, tokv=TOKV, rtok=RTOK,
                     forget=FORGET, fstage=FSTAGE, resplit=RESPLIT, yout=YOUT)
        sems = {(k, e): sem(f"{k}_{e}") for k, v in kinds.items() for e in v}
        nxt = {(k, e): PRIME * len(kinds[k][e]) for k, e in sems}

        def run(kind, n=1):
            out = {}
            for e, names in kinds[kind].items():
                out[e] = Steps(sems[kind, e], names, nxt[kind, e])
                nxt[kind, e] += n * len(names)
            return out

        def prime(eng, name):
            for (k, e), s in sems.items():
                if e == name:
                    eng.sem_inc(s, PRIME * len(kinds[k][e]))

        unit = [0]
        size = {}

        def units(n, *sizes):
            for u in range(n):
                size[unit[0] + u] = sizes[u % len(sizes)]
            unit[0] += n
            return unit[0] - n

        def ffn(f, gain):
            parts = []
            for hf in range(HALVES):
                kind = "honly" if hf == 0 else "last" if gain is None else "update"
                parts.append(dict(kind="in", u=units(2 * FT, KC * P), st=run("ffn", FT), f=f, half=hf,
                                  x=None, rms=None))
                parts.append(dict(kind="out", what=kind, u=units(KC, FT * P), kt=FT, scale=0.5,
                                  st=run(kind, KC), src=("ffn", f, hf), gain=gain, first=None))
            return parts

        X0 = run("xsplit", KC)
        F0 = ffn(0, G_MIX)
        F0[0].update(x=X0, rms=run("rms"))
        Z = dict(u=units(4, 4 * ZW // 2), x=F0[3]["st"], rms=run("rms"), st=run("latent"))
        M = dict(u=units(2 * PAIRS, QC * 2 * DA, LC * 4 * DV), d=DA, proj=run("proj", PAIRS),
                 stage=run("stage", PAIRS), stagev=run("stagev", PAIRS), head0=run("head0", PAIRS),
                 att=run("att", PAIRS))
        MO = dict(kind="out", what="update", u=units(KC, KC * P), kt=KC, scale=1.0, st=run("update", KC),
                  src=("a",), gain=G_FFN + 8, first=M)
        F1 = ffn(1, G_BKV)
        F1[0].update(x=MO["st"], rms=run("rms"))
        KV = dict(u=units(16, 2 * 512), x=F1[3]["st"], rms=run("rms"), rtok=run("rtok"),
                  k=[run("tokn"), run("tokn")], v=[run("tokv"), run("tokv")], forget=run("forget"),
                  resplit=run("resplit", KC))
        F2 = ffn(2, G_MIX + 8)
        F2[0].update(x=KV["resplit"])
        Q = dict(u=units(8, 2 * 512), x=F2[3]["st"], rms=run("rms"), rtok=run("rtok"),
                 k=[run("tokq"), run("tokq1")])
        X = dict(d=DBX, stage=run("stage", PAIRS), stagev=run("stagev", PAIRS), head0=run("head0", PAIRS),
                 att=run("att", PAIRS), fstage=run("fstage", PAIRS))
        XO = dict(kind="out", what="update", u=units(KC, KC * P), kt=KC, scale=1.0, st=run("update", KC),
                  src=("b",), gain=G_FFN + 24, first=X)
        F3 = ffn(3, None)
        F3[0].update(x=XO["st"], rms=run("rms"))
        Y = dict(x=F3[3]["st"], rms=run("rms"), yout=run("yout", KC))
        xf = [arena[:, k * T:(k + 1) * T] for k in range(KC)]
        block = ctx.enter_context(nc.Block())

        def w_uses(L, p, attends, stages, projects, mla):
            def turned(hh):
                return [(f"t{hh}{j}", p, attends, [("att", "dve", f"pt{hh}{j}")]) for j in range(4)]

            every = turned(0)
            every += [(n, p + 1, stages, [("stage", "dve", s)])
                      for n, s in (("tq0", "q0"), ("tq1", "q1"), ("tp0", "p0"), ("tp1", "p1"), ("tc0", "c0"),
                                   ("tc1", "c1"), ("ts", "sk"))]
            every += turned(1)
            if mla:
                every += [(f"q{n}", p + 2, projects, [("proj", "dve", f"q{n}")]) for n in range(3)]
                every += [(f"kv{n}", p + 2, projects, [("proj", "dve", f"v{n}")]) for n in range(5)]
            turns = [x for x in every if x[0] != "tp1"]
            bank = {x[0]: W_BANKS[n % 3] for n, x in enumerate(turns)} | {"tp1": 0}
            return [(name, bank[name], it, readers) for name, it, takes, readers in every if takes]

        @block.sync
        def _(sp):
            def load(par, u, src, n):
                sp.wait_ge(w_lo, u + 1)
                sp.dma_start(raw[par][:, 0:n], src).then_inc(w_load[par], 16)

            def load_two(q, i):
                for j in range(2):
                    if q["src"][0] == "ffn":
                        src = d["w_ffn_out"][q["src"][1], q["src"][2], 2 * i + j]
                    else:
                        src = d["w_a_out" if q["src"][0] == "a" else "w_b_out"][2 * i + j]
                    load(j, q["u"] + 2 * i + j, src, q["kt"] * P)

            def load_out(q, first=0):
                with sp.Fori(first, KC // 2) as i:
                    load_two(q, i)

            def load_ffn(fs):
                for q in fs:
                    if q["kind"] == "in":
                        with sp.Fori(0, FT) as i:
                            for j in range(2):
                                load(j, q["u"] + 2 * i + j, d["w_ffn_in"][q["f"], q["half"], i, j], KC * P)
                    else:
                        load_out(q)

            sp.dma_start(gc[:, :], d["g_cols"]).then_inc(loaded["gains"], 16)
            n = KC * T // X_PARTS
            for k in range(X_PARTS):
                sp.dma_start(h[:, k * n:(k + 1) * n], d["x"][:, k * n:(k + 1) * n]).then_inc(loaded["x"][k], 16)
                if k == 0:
                    load(0, F0[0]["u"], d["w_ffn_in"][0, 0, 0, 0], KC * P)
            load(1, F0[0]["u"] + 1, d["w_ffn_in"][0, 0, 0, 1], KC * P)
            for dst, src in ((ident[:, :], d["c_ident"]),
                             (gq[0:DA, :], d["g_a_qk"][0]), (gk[0:DA, :], d["g_a_qk"][1]),
                             (gbq[0:DB, :], d["g_b_qn"])):
                sp.dma_start(dst, src).then_inc(loaded["const"], 16)
            with sp.Fori(1, FT) as i:
                for j in range(2):
                    load(j, F0[0]["u"] + 2 * i + j, d["w_ffn_in"][0, 0, i, j], KC * P)
            for dst, src in ((cos_sin[:, :, :, :], d["c_rope"]), (kpe[:, NT:NK, :], d["kpe"]),
                             (cached_raw, d["lat_T"]), (gkv, d["g_a_kv"].to_broadcast([P, KV_RANK])),
                             (mask_tmp, d["c_mask_chunk"])):
                sp.dma_start(dst, src).then_inc(loaded["mla"], 16)
            load_ffn(F0[1:])
            for c in range(2):
                for k in range(2):
                    load(k, Z["u"] + 2 * c + k, d["w_a_in"][c, k], 4 * ZW // 2)
            load(0, M["u"], d["w_a_qup"][0], QC * 2 * DA)
            load(1, M["u"] + 1, d["w_a_kvup"][0], LC * 4 * DV)
            sp.wait_ge(*Z["st"]["dve"].at("lat4"))
            o_lat = d["o_lat_p"].rearrange("(t p) w -> p t w", p=P)
            sp.dma_start(o_lat, lat[:, 0:4, Q_RANK:Q_RANK + KV_RANK]).then_inc(stored, 16)
            sp.dma_start(d["o_lat_s"], lat[S0:P, 4, Q_RANK:Q_RANK + KV_RANK]).then_inc(stored, 16)
            sp.dma_start(d["o_kpe_p"].rearrange("(t p) w -> p t w", p=P), kpe[:, 0:4, :]).then_inc(stored, 16)
            sp.dma_start(d["o_kpe_s"], kpe[S0:P, 4, :]).then_inc(stored, 16)
            with sp.Fori(1, PAIRS) as i:
                load(0, M["u"] + 2 * i, d["w_a_qup"][i], QC * 2 * DA)
                load(1, M["u"] + 2 * i + 1, d["w_a_kvup"][i], LC * 4 * DV)
            load_out(MO)
            load_ffn(F1[:1])
            sp.wait_ge(stored, 64)
            for dst, src in ((gkn[:, :], d["g_b_kn"].to_broadcast([P, DB])),
                             (bf[:, :], d["b_b_f"].to_broadcast([P, HEADS])), (mask_raw[:, :], d["c_mask_causal"]),
                             (wf[:, :], d["w_f"]), (tri[:, :], d["c_tri"]), (lf[:, NT:NK, :], d["logf"])):
                sp.dma_start(dst, src).then_inc(loaded["fox"], 16)
            load_ffn(F1[1:])

            for c in range(4):
                for k in range(4):
                    load(k % 2, KV["u"] + 4 * c + k, d["w_b_kv"][c, k], 2 * 512)
            load_ffn(F2)
            for c in range(2):
                for k in range(4):
                    load(k % 2, Q["u"] + 4 * c + k, d["w_b_q"][c, k], 2 * 512)
            load_two(XO, 0)
            ksx = ks[:, 0:NK * 2 * DBX].rearrange("p (t g w) -> p t g w", t=NK, g=2)
            vsx = vr.rearrange("p (t g w) -> p t g w", t=NK, g=2)
            for s in range(2):
                sp.wait_ge(stored_kv[s], 64)
            sp.wait_ge(*KV["k"][1]["dve"].at("ss"))
            def load_heads(p, loaded_, new_p, new_s, old, dst):
                for g in range(2):
                    cols = bass.ds(p * 2 * DB + g * DB, DB)
                    sp.dma_start(dst[:, 0:4, g, 0:DB], d[new_p].rearrange("(t p) e -> p t e", p=P)[:, :, cols]
                                 ).then_inc(loaded_, 16)
                    sp.dma_start(dst[S0:P, 4, g, 0:DB], d[new_s][:, cols]).then_inc(loaded_, 16)
                    sp.dma_start(dst[:, NT:NK, g, 0:DB], d[old].rearrange("(t p) e -> p t e", p=P)[:, :, cols]
                                 ).then_inc(loaded_, 16)

            with sp.Fori(0, PAIRS) as p:
                sp.wait_ge(*X["stage"]["pe"].at("ts", p - 1))
                load_heads(p, k_loaded, "o_k_p", "o_k_s", "fox_k", ksx)
                sp.wait_ge(*X["stagev"]["pool"].at("v", p - 1))
                load_heads(p, v_loaded, "o_v_p", "o_v_s", "fox_v", vsx)
            load_out(XO, 1)
            load_ffn(F3)
            for k in range(KC):
                sp.wait_ge(*Y["yout"]["dve"].at("y", k))
                sp.dma_start(d["o_y"][k], xf[k]).then_inc(stored, 16)
            sp.wait_ge(stored, 16 * (4 + KC))
            sp.wait_ge(stored_lf, 32)
            for s in range(2):
                sp.wait_ge(stored_kv[s], 64)

        @block.tensor
        def _(pe):
            prime(pe, "pe")
            pe.sem_inc(w_used, PRIME)

            def product(out, lhs, rhs, start, stop):
                pe.matmul(out, lhs[0], rhs[0], start=start, stop=False)
                pe.matmul(out, lhs[0], rhs[1], start=False, stop=False)
                return pe.matmul(out, lhs[1], rhs[0], start=False, stop=stop)

            def unit_ready(u):
                pe.wait_ge(w_lo, u + PRIME + 1)

            def sum_squares(x, k):
                pe.wait_ge(*x["act"].at("sq", k))
                for n in range(2):
                    mm = pe.matmul(pair(1)[:, n, :], ones[:, :], scratch[k % 2][:, n * HALF_T:(n + 1) * HALF_T],
                                   start=(k == 0), stop=(k == KC - 1))
                mm.then_inc(x["pe"].sem, 1)

            def wide(bank, par, kt, xs, each):
                for k in range(kt):
                    if each is not None:
                        each(k)
                    w = [t[par][:, k * P:(k + 1) * P] for t in (wh, wl)]
                    for n in range(2):
                        cols = slice(k * T + n * HALF_T, k * T + (n + 1) * HALF_T)
                        mm = product(pair(bank)[:, n, :], w, [t[:, cols] for t in xs], k == 0, k == kt - 1)
                mm.then_inc(w_used, 1)

            def ffn_in(q):
                st = q["st"]["dve"]

                def tile_pair(i, first):
                    def each(k):
                        if q["x"] is not None:
                            if q["rms"] is not None and (k == KC - 1 or q["x"] is X0):
                                sum_squares(q["x"], k)
                            pe.wait_ge(*q["x"]["dve"].at("x_lo", k))

                    unit_ready(q["u"] + 2 * i)
                    pe.wait_ge(*st.at("gate", i - 1))
                    wide(0, 0, KC, xa, each if first else None)
                    unit_ready(q["u"] + 2 * i + 1)
                    pe.wait_ge(*st.at("up", i - 1))
                    if first and q["rms"] is not None:
                        pe.wait_ge(*q["rms"]["act"].at("sd"))
                    wide(1, 1, KC, xa, None)

                tile_pair(0, True)
                with pe.Fori(1, FT) as i:
                    tile_pair(i, False)

            def out_proj(q, before=None):
                st = q["st"]

                def tile_of(i, j, first):
                    dd = 2 * i + j
                    unit_ready(q["u"] + dd)
                    pe.wait_ge(*st["dve"].at("h", dd - 2))
                    each = None
                    if first and j == 0:
                        if before is not None:
                            def each(k):
                                pe.wait_ge(*before["st"]["dve"].at("hid_lo", k))
                        else:
                            pe.wait_ge(*q["first"]["att"]["dve"].at("o", PAIRS - 1))
                    wide(2 + j, j, q["kt"], hid, each)
                    if q["what"] != "honly" and not (first and j == 0):
                        pe_sum(i, j, first)

                def pe_sum(i, j, first):
                    pe.wait_ge(*st["act"].at("sq", 2 * i + j - 1))
                    for n in range(2):
                        mm = pe.matmul(pair(1)[:, n, :], ones[:, :],
                                       scratch[(j + 1) % 2][:, n * HALF_T:(n + 1) * HALF_T],
                                       start=(first and j == 1), stop=False)
                    mm.then_inc(st["pe"].sem, 1)

                for j in range(2):
                    tile_of(0, j, True)
                with pe.Fori(1, KC // 2) as i:
                    for j in range(2):
                        tile_of(i, j, False)

            def ffn_all(fs):
                for q in fs:
                    if q["kind"] == "in":
                        before = q
                        ffn_in(q)
                    else:
                        out_proj(q, before)

            def tok_unit(u, c, k0, kn, n, bank_free):
                unit_ready(u)
                for t in range(NT):
                    if k0 == 0:
                        bank_free(c, t)
                    out = ps[:, TOK_BANKS[(NT * c + t) % 7], 0:n]
                    for k in range(kn):
                        x = [a[:, (k0 + k) * T + TS[t]:(k0 + k) * T + TS[t] + P] for a in xa]
                        w = [a[u % 2][:, k * n:(k + 1) * n] for a in (wh, wl)]
                        mm = product(out, x, w, k0 + k == 0, k0 + k == KC - 1)
                mm.then_inc(w_used, 1)

            def token_rstd(rms, step):
                pe.wait_ge(*rms["dve"].at("r"))
                for t in range(NT):
                    mm = pe.matmul(ps[:, MISC, t:t + 1], rstd[0:1, TS[t]:TS[t] + P], ones[0:1, 0:1],
                                   start=True, stop=True)
                mm.then_inc(step.sem, 1)

            pe.wait_ge(set_dve, 5)
            ffn_all(F0)

            def z_free(c, t):
                if c == 0 and t == 0:
                    pe.wait_ge(*Z["x"]["dve"].at("h", KC - 1))
                elif NT * c + t >= 7:
                    pe.wait_ge(*Z["st"]["dve"].at(f"z0{NT * c + t - 7}"))
                elif TOK_BANKS[(NT * c + t) % 7] == 2:
                    pe.wait_ge(*Z["rms"]["act"].at("sd"))

            for c in range(2):
                for k in range(2):
                    pe.wait_ge(*Z["x"]["dve"].at("x_lo", 4 * k + 3))
                    tok_unit(Z["u"] + 2 * c + k, c, 4 * k, 4, ZW // 2, z_free)
                    if c == 0 and k == 0:
                        sum_squares(Z["x"], KC - 1)
                    if c == 0 and k == 1:
                        token_rstd(Z["rms"], Z["st"]["pe"])
            st = Z["st"]
            pe.wait_ge(*st["dve"].at("lat4"))
            for j in range(QC + LC):
                for t in range(4):
                    mm = pe.transpose(ps[:, j, t * P:(t + 1) * P], lat[:, t, j * P:(j + 1) * P], ident[:, :])
                mm.then_inc(st["pe"].sem, 1)
            for j in range(QC + LC):
                mm = pe.transpose(ps[:, 5, j * DEC:(j + 1) * DEC], lat[S0:P, 4, j * P:(j + 1) * P],
                                  ident[S0:P, S0:P])
            mm.then_inc(st["pe"].sem, 1)

            def attention(L, mla, mask):
                att, stg, D = L["att"], L["stage"], L["d"]
                prj = L.get("proj")
                qsv = qs[:, 0:NT * 2 * D].rearrange("p (t g w) -> p t g w", t=NT, g=2)
                ksv = ks[:, 0:NK * 2 * D].rearrange("p (t g w) -> p t g w", t=NK, g=2)

                def bank_of(name, uses, before):
                    n = [x[0] for x in uses].index(name)
                    b = uses[n][1]
                    if name == "tp1":
                        pe.wait_ge(*L["att"]["act"].at("exp13", uses[n][2] - 1))
                    past = [x for x in before + uses[:n] if x[1] == b]
                    if past:
                        _, _, it, readers = past[-1]
                        for k, e, s in readers:
                            pe.wait_ge(*L[k][e].at(s, it))
                    return b

                def project_q(it, uses, before):
                    unit_ready(M["u"] + 2 * it)
                    for n in range(3):
                        b = bank_of(f"q{n}", uses, before)
                        for t in range(2 * n, min(2 * n + 2, NT)):
                            for k in range(QC):
                                mm = product(ps[:, b, (t % 2) * 2 * DA:(t % 2 + 1) * 2 * DA],
                                             [a[:, k * T + TS[t]:k * T + TS[t] + P] for a in cqT],
                                             [a[0][:, k * 2 * DA:(k + 1) * 2 * DA] for a in (wh, wl)],
                                             k == 0, k == QC - 1)
                        mm.then_inc(prj["pe"].sem if n < 2 else w_used, 1)

                def project_kv(it, uses, before):
                    unit_ready(M["u"] + 2 * it + 1)
                    for n in range(5):
                        b = bank_of(f"kv{n}", uses, before)
                        for t in range(2 * n, min(2 * n + 2, NK)):
                            for k in range(LC):
                                mm = product(ps[:, b, (t % 2) * 4 * DV:(t % 2 + 1) * 4 * DV],
                                             [a[:, k * KEYS + KSTART[t]:k * KEYS + KSTART[t] + P] for a in latT],
                                             [a[1][:, k * 4 * DV:(k + 1) * 4 * DV] for a in (wh, wl)],
                                             k == 0, k == LC - 1)
                        mm.then_inc(prj["pe"].sem if n < 4 else w_used, 1)

                def turn_staged(it, uses, before, between=None):
                    if mla:
                        pe.wait_ge(*prj["pool"].at("kpe", it))
                        pe.wait_ge(*prj["dve"].at("kn", it))
                    else:
                        pe.wait_ge(*L["fstage"]["pool"].at("ck", it))
                        pe.wait_ge(k_loaded, 16 * 6 * (it + 1))
                    sem_ = stg["pe"].sem
                    for name, v, t0 in (("tq", qsv, 0), ("tp", ksv, 0), ("tc", ksv, NT)):
                        for g in range(2):
                            b = bank_of(f"{name}{g}", uses, before)
                            for t in range(4):
                                if name == "tc" and g == 1 and t == 3:
                                    b_ts = bank_of("ts", uses, before)
                                mm = pe.transpose(ps[0:D, b, t * P:(t + 1) * P], v[:, t0 + t, g, :], ident[:, :])
                            mm.then_inc(sem_, 1)
                            if (name, g) == ("tp", 0) and between is not None:
                                between()
                    b = b_ts
                    for n, v in enumerate((qsv, ksv)):
                        for g in range(2):
                            o = (2 * n + g) * DEC
                            mm = pe.transpose(ps[0:D, b, o:o + DEC], v[S0:P, 4, g, :], ident[S0:P, S0:P])
                    mm.then_inc(sem_, 1)

                def scores(hh, u, p):
                    if u < 3:
                        pe.wait_ge(*(att["act"].at(f"exp1{3 if u == 0 else 4}", p - 1) if hh == 0
                                     else L["head0"]["act"].at(f"exp0{3 if u == 0 else 4}", p)))
                    else:
                        pe.wait_ge(*L["head0" if hh == 0 else "att"]["act"].at(f"exp{hh}{0 if u == 3 else 2}", p))
                    if hh == 0 and u == 0:
                        pe.wait_ge(*stg["dve"].at("sk", p))
                    q = [a[0:D, hh * T + TS[u]:hh * T + TS[u] + P] for a in qT]
                    k = [a[0:D, hh * KEYS:(hh + 1) * KEYS] for a in kT]
                    if u < 4:
                        out = ps[:, u % 3, 0:P_W[u]]
                        product(out, q, [a[:, 0:P_W[u]] for a in k], True, False)
                        mm = pe.matmul(out[:, u * P:(u + 1) * P], identr[:, :], mask[:, :], start=False, stop=True)
                    else:
                        for n in range(2):
                            c = SEQ + n * HALF_T
                            mm = product(ps[:, 1 + n, 0:HALF_T], q, [a[:, c:c + HALF_T] for a in k], True,
                                         mla or n == 0)
                        if not mla:
                            mm = pe.matmul(ps[:, 2, HALF_T - DEC:HALF_T], identr[:, :], mask[:, S0:P],
                                           start=False, stop=True)
                    mm.then_inc(L["head0" if hh == 0 else "att"]["pe"].sem, 1)

                def turn(hh, j, p, uses, before):
                    if j in (0, 3):
                        pe.wait_ge(*L["head0" if hh == 0 else "att"]["pool"].at(f"d{hh}{3 if j == 0 else 4}", p))
                    b = bank_of(f"t{hh}{j}", uses, before)
                    first = PT_S if (hh, j) == (0, 3) else 0
                    for u in range(j, 4):
                        mm = pe.matmul(ps[:, b, first + (u - j) * P:first + (u - j + 1) * P],
                                       prob[:, P_OFF[u] + j * P:P_OFF[u] + (j + 1) * P], diag[u], start=True, stop=True)
                    if j == 3:
                        for jj in range(5):
                            o = P_OFF[4] + (jj * P if jj < 4 else P_W[4] - P)
                            to = (P if hh == 1 else 0) + jj * DEC
                            mm = pe.matmul(ps[:, b, to:to + DEC], prob[S0:P, o:o + P],
                                           diag[4][S0:P, S0:P], start=True, stop=True)
                    mm.then_inc(att["pe"].sem, 1)

                def values(hh, p):
                    if hh == 0:
                        pe.wait_ge(*L["stagev"]["pool"].at("v", p))
                        pe.wait_ge(*att["dve"].at("o", p - 1))
                    pe.wait_ge(*att["dve"].at(f"pt{hh}3", p))
                    c = slice(hh * DV, hh * DV + P)
                    for j in range(4):
                        mm = product(ps[:, 6, j * P:SEQ], [a[:, j, c] for a in vT],
                                [a[:, PT_OFF[j]:PT_OFF[j] + PT_W[j]] for a in pT], hh == 0 and j == 0,
                                hh == 1 and j == 3)
                    if hh == 1:
                        for jj in range(5):
                            r0, t = (0, 1 + jj) if jj < 4 else (S0, 0)
                            x = [a[r0:P, :, jj * DEC:(jj + 1) * DEC] for a in pS]
                            mm = product(ps[:, 7, 0:2 * DEC].rearrange("p (g w) -> p g w", g=2),
                                         [a[r0:P, t, :] for a in vsT], x, jj == 0, jj == 4)
                    mm.then_inc(att["pe"].sem, 1)

                def turn_of(p, stages, projects):
                    uses = w_uses(L, p, True, stages, projects, mla)
                    before = w_uses(L, p - 1, True, True, stages, mla)
                    for j in range(4):
                        turn(0, j, p, uses, before)
                        scores(1, j, p)
                    scores(1, 4, p)
                    if stages and not mla:
                        turn_staged(p + 1, uses, before, lambda: values(0, p))
                    else:
                        values(0, p)
                        if stages:
                            turn_staged(p + 1, uses, before)
                    for j in range(4):
                        turn(1, j, p, uses, before)
                        if stages:
                            scores(0, j, p + 1)
                    if stages:
                        scores(0, 4, p + 1)
                    values(1, p)
                    if mla and projects:
                        project_q(p + 2, uses, before)
                        project_kv(p + 2, uses, before)

                first = [w_uses(L, -2, False, False, True, mla), w_uses(L, -1, False, True, True, mla)]
                if mla:
                    pe.wait_ge(*Z["st"]["dve"].at("u4"))
                    project_q(0, first[0], [])
                    project_kv(0, first[0], [])
                turn_staged(0, first[1], first[0])
                for u in range(5):
                    scores(0, u, 0)
                if mla:
                    project_q(1, first[1], first[0])
                    project_kv(1, first[1], first[0])
                with pe.Fori(0, PAIRS - 2) as p:
                    turn_of(p, True, True)
                turn_of(PAIRS - 2, True, False)
                turn_of(PAIRS - 1, False, False)

            attention(M, True, mask_chunk)
            out_proj(MO)
            ffn_all(F1)

            def kv_free(c, t):
                n = NT * c + t
                if n == 0:
                    pe.wait_ge(*KV["x"]["dve"].at("h", KC - 1))
                elif n in (5, 6):
                    pe.wait_ge(*KV["forget"]["dve"].at(f"fs{n - 5}"))
                elif n >= 7:
                    c0, t0 = divmod(n - 7, NT)
                    pe.wait_ge(*(KV["k"][c0] if c0 < 2 else KV["v"][c0 - 2])["dve"].at(f"c{t0}"))

            for m in range(16):
                if m < 4:
                    pe.wait_ge(*KV["x"]["dve"].at("x_lo", 2 * m + 1))
                tok_unit(KV["u"] + m, m // 4, 2 * (m % 4), 2, 512, kv_free)
                if m == 0:
                    sum_squares(KV["x"], KC - 1)
                if m == 2:
                    token_rstd(KV["rms"], KV["rtok"]["pe"])
                if m == 3:
                    pe.wait_ge(*KV["rtok"]["dve"].at("rtok"))
                    pe.wait_ge(*KV["forget"]["dve"].at("wlo"))
                    for k in range(KC):
                        w = [a[:, k * HEADS:k * HEADS + P] for a in wfs]
                        for n in range(2):
                            x = [a[:, k * T + n * HALF_T:k * T + (n + 1) * HALF_T] for a in xa]
                            mm = product(ps[:, F_BANKS[n], 0:HALF_T], w, x, k == 0, k == KC - 1)
                    mm.then_inc(KV["forget"]["pe"].sem, 1)
                if m == 4:
                    pe.wait_ge(*KV["forget"]["dve"].at("fs1"))
                    for t in range(NT):
                        mm = pe.transpose(ps[:, MISC, 16 + t * HEADS:16 + (t + 1) * HEADS],
                                          fT[:, TS[t]:TS[t] + P], ident[0:HEADS, 0:HEADS])
                    mm.then_inc(KV["forget"]["pe"].sem, 1)
                if m == 9:
                    pe.wait_ge(*KV["forget"]["dve"].at("lf"))
                    for t in range(NK):
                        o = ps[:, MISC, 128 + t * HEADS:128 + (t + 1) * HEADS]
                        past = range(t) if t < 4 else range(NT, NK) if t == 4 else range(NT, t)
                        for n, s in enumerate(past):
                            pe.matmul(o, ones[:, :], lf[:, s, :], start=(n == 0), stop=False)
                        r0 = S0 if t == 4 else 0
                        mm = pe.matmul(o, tri[r0:P, :], lf[r0:P, t, :], start=len(past) == 0, stop=True)
                    mm.then_inc(KV["forget"]["pe"].sem, 1)
            pe.wait_ge(*KV["v"][1]["dve"].at("c4"))
            ffn_all(F2)

            def q_free(c, t):
                n = NT * c + t
                if n == 0:
                    pe.wait_ge(*Q["x"]["dve"].at("h", KC - 1))
                elif n >= 7:
                    pe.wait_ge(*Q["k"][0]["dve"].at(f"c{n - 7}"))
                elif n == 6:
                    pe.wait_ge(*Q["rms"]["act"].at("sd"))

            for m in range(8):
                if m < 4:
                    pe.wait_ge(*Q["x"]["dve"].at("x_lo", 2 * m + 1))
                tok_unit(Q["u"] + m, m // 4, 2 * (m % 4), 2, 512, q_free)
                if m == 0:
                    sum_squares(Q["x"], KC - 1)
                if m == 2:
                    token_rstd(Q["rms"], Q["rtok"]["pe"])
            pe.wait_ge(*Q["k"][1]["dve"].at("c4"))
            attention(X, False, mask_causal)
            out_proj(XO)
            ffn_all(F3)
            sum_squares(Y["x"], KC - 1)

        @block.scalar
        def _(act):
            prime(act, "act")

            def split_hi(par, u, loads, n):
                act.wait_ge(w_load[par], 16 * loads)
                act.wait_ge(w_used, u + 1)
                act.activation(wh[par][:, 0:n], raw[par][:, 0:n], ACT.Copy).then_inc(w_hi, 1)

            def ahead(u):
                if u < unit[0]:
                    split_hi(u % 2, u, u // 2 + 1, size[u])

            def root(rms, x):
                act.wait_ge(*x["pe"].at("stat", KC - 1))
                act.activation(two(scratch[2]), pair(1), ACT.Sqrt, bias=eps[:, 0:1], scale=1.0 / D_MODEL
                               ).then_inc(rms["act"].sem, 1)

            def split_x(k, dve_h, x, gain, par):
                if dve_h is not None:
                    act.wait_ge(*dve_h)
                act.wait_ge(*x["pe"].at("stat", k - 2))
                act.activation(tile(xa[0], k), tile(h, k), ACT.Copy, scale=gc[:, bass.ds(gain + k, 1)]
                               ).then_inc(x["act"].sem, 1)
                act.activation(scratch[par], tile(h, k), ACT.Square).then_inc(x["act"].sem, 1)

            def ffn_in(q):
                st, U = q["st"], q["u"]

                def turn(i, n_next, first):
                    split_hi(1, U + 2 * i + 1, U // 2 + i + 1, KC * P)
                    if first and q["rms"] is not None:
                        root(q["rms"], q["x"])
                    act.wait_ge(*st["dve"].at("gate", i))
                    act.activation(scratch[2], scratch[0], ACT.Silu).then_inc(st["act"].sem, 1)
                    split_hi(0, U + 2 * i + 2, U // 2 + i + 2, n_next)
                    act.wait_ge(*st["dve"].at("hid", i))
                    act.activation(tile(hid[0], i), scratch[3], ACT.Copy).then_inc(st["act"].sem, 1)

                turn(0, KC * P, True)
                with act.Fori(1, FT - 1) as i:
                    turn(i, KC * P, False)
                turn(FT - 1, size[U + 2 * FT], False)

            def out_proj(q):
                st, U, n = q["st"], q["u"], q["kt"] * P

                def turn(i, last):
                    for j in range(2):
                        if last and j == 1:
                            ahead(U + KC)
                        else:
                            split_hi((j + 1) % 2, U + 2 * i + j + 1, (U + j + 1) // 2 + i + 1, n)
                        if q["what"] == "update":
                            split_x(2 * i + j, st["dve"].at("h", 2 * i + j), st, q["gain"], j)
                        elif q["what"] == "last":
                            act.wait_ge(*st["dve"].at("h", 2 * i + j))
                            act.wait_ge(*st["pe"].at("stat", 2 * i + j - 2))
                            act.activation(scratch[j], tile(h, 2 * i + j), ACT.Square).then_inc(st["act"].sem, 1)

                with act.Fori(0, KC // 2 - 1) as i:
                    turn(i, False)
                turn(KC // 2 - 1, True)

            def ffn_all(fs):
                for q in fs:
                    ffn_in(q) if q["kind"] == "in" else out_proj(q)

            act.wait_ge(loaded["gains"], 16)
            for k in range(KC):
                act.wait_ge(loaded["x"][k * X_PARTS // KC], 16)
                split_x(k, None, X0, G_FFN, k % 2)
                if k == 0:
                    ahead(0)
            act.wait_ge(loaded["const"], 64)
            act.wait_ge(set_dve, 7)
            act.activation(identr[:, :], ident[:, :], ACT.Copy).then_inc(set_act, 1)
            ffn_all(F0)

            for m in range(4):
                ahead(Z["u"] + m + 1)
                if m == 0:
                    root(Z["rms"], Z["x"])
            st = Z["st"]
            inc = st["act"].sem
            act.wait_ge(*st["dve"].at("z14"))
            for o, w, col, name in ((0, Q_RANK, ST_MS, "sq"), (Q_RANK, KV_RANK, ST_MS + 5, "sk")):
                for t in range(NT):
                    if (name, t) != ("sq", 0):
                        act.wait_ge(*st["act"].at(f"{name}{t - 1}" if t else "sq4"))
                    act.activation(scratch[0][:, 0:w], lat[:, t, o:o + w], ACT.Square,
                                   accum_out=stat[:, col + t:col + t + 1]).then_inc(inc, 1)
            act.wait_ge(*st["act"].at("sk4"))
            act.activation(stat[:, ST_MS + 10:ST_MS + 15], stat[:, ST_MS:ST_MS + 5], ACT.Sqrt, bias=eps[:, 0:1],
                           scale=1.0 / Q_RANK).then_inc(inc, 1)
            act.activation(stat[:, ST_MS + 15:ST_MS + 20], stat[:, ST_MS + 5:ST_MS + 10], ACT.Sqrt,
                           bias=eps[:, 0:1], scale=1.0 / KV_RANK).then_inc(inc, 1)
            act.wait_ge(loaded["mla"], 80)
            act.wait_ge(*st["dve"].at("rope"))
            act.activation(scratch[3][:, 0:NK * ROPE], kpe[:, :, :].rearrange("p t w -> p (t w)"), ACT.Square
                           ).then_inc(inc, 1)
            new = latT[0][:, :].rearrange("p (j w) -> p j w", j=LC)
            act.activation(new[:, :, SEQ:SEQ + PAST], cached_raw.rearrange("p (j w) -> p j w", j=LC), ACT.Copy
                           ).then_inc(inc, 1)
            act.activation(mask_chunk[:, :], mask_tmp, ACT.Copy).then_inc(inc, 1)
            for j in range(QC + LC):
                act.wait_ge(*st["pe"].at(f"t{j}"))
                if j < QC:
                    act.activation(cqT[0][:, j * T:j * T + SEQ], ps[:, j, :], ACT.Copy,
                                   scale=gc[:, G_AQ + j:G_AQ + j + 1]).then_inc(inc, 1)
                else:
                    act.activation(latT[0][:, (j - QC) * KEYS:(j - QC) * KEYS + SEQ], ps[:, j, :], ACT.Copy
                                   ).then_inc(inc, 1)
            act.wait_ge(*st["pe"].at("t5"))
            for j in range(QC + LC):
                src = ps[:, 5, j * DEC:(j + 1) * DEC]
                if j < QC:
                    act.activation(cqT[0][:, j * T + SEQ:(j + 1) * T], src, ACT.Copy,
                                   scale=gc[:, G_AQ + j:G_AQ + j + 1]).then_inc(inc, 1)
                else:
                    act.activation(latT[0][:, (j - QC) * KEYS + SEQ + PAST:(j - QC + 1) * KEYS], src, ACT.Copy
                                   ).then_inc(inc, 1)

            def attention(L, mla, g_q, g_k):
                att, stg, D, U = L["att"], L["stage"], L["d"], L.get("u")
                prj = L.get("proj")
                banks = {n: b for n, b, _, _ in w_uses(L, 0, True, True, True, mla)}

                def exp(hh, u, p):
                    r0 = S0 if u == 4 else 0
                    c = 5 * hh + u
                    src = ps[S0:P, 1:3, 0:HALF_T] if u == 4 else ps[:, u % 3, 0:P_W[u]]
                    st = L["head0" if hh == 0 else "att"]
                    act.wait_ge(*st["dve"].at(f"m{hh}{u}", p))
                    act.wait_ge(*att["pe"].at(f"t{1 - hh}{min(u, 3)}", p - 1 if hh == 0 else p))
                    dst = prob[r0:P, P_OFF[u]:P_OFF[u] + P_W[u]]
                    act.activation(two(dst) if u == 4 else dst, src, ACT.Exp, bias=stat[r0:P, ST_NM + c:ST_NM + c + 1],
                                   accum_out=stat[r0:P, ST_RS + c:ST_RS + c + 1]).then_inc(st["act"].sem, 1)

                def split_p(hh, j, p):
                    o, w = (PT_OFF[j], PT_W[j]) if j < 3 else (PS_OFF[0] if hh == 0 else PT_OFF[3], PT_W[3] + PT_S)
                    act.wait_ge(*att["pe"].at(f"t{hh}{j}", p))
                    if j == 0:
                        act.wait_ge(*att["pe"].at(f"pv{1 - hh}", p - 1 if hh == 0 else p))
                    act.activation(pT[0][:, o:o + w], ps[:, banks[f"t{hh}{j}"], 0:w], ACT.Copy
                                   ).then_inc(att["act"].sem, 1)

                def project(it):
                    inc = prj["act"].sem
                    act.wait_ge(*prj["dve"].at("rope", it))
                    act.activation(scr[:, NK * 2 * NOPE:NK * 2 * NOPE + nq], qs, ACT.Square).then_inc(inc, 1)
                    for n in range(5):
                        if n < 4:
                            act.wait_ge(*prj["pe"].at(f"kv{n}", it))
                        else:
                            act.wait_ge(w_used, U + 2 * it + 1 + PRIME + 1)
                        if n == 0:
                            act.wait_ge(*stg["pe"].at("ts", it - 1))
                        w = 2 if n < 4 else 1
                        src = ps[:, banks[f"kv{n}"], 0:w * 4 * DV].rearrange("p (t x) -> p t x", t=w)
                        dst = ks.rearrange("p (t g w) -> p t g w", t=NK, g=2)
                        act.activation(dst[:, 2 * n:2 * n + w, :, 0:NOPE],
                                       src[:, :, 0:2 * NOPE].rearrange("p t (g w) -> p t g w", g=2), ACT.Copy
                                       ).then_inc(inc, 1)

                def square_keys(it):
                    act.wait_ge(*prj["act"].at("k4", it))
                    act.activation(scr[:, 0:NK * 2 * NOPE].rearrange("p (t w) -> p t w", w=NOPE),
                                   ks.rearrange("p (t w) -> p t w", w=DA)[:, :, 0:NOPE], ACT.Square
                                   ).then_inc(prj["act"].sem, 1)

                def stage_values(it):
                    act.wait_ge(*att["pe"].at("pv1", it - 1))
                    if mla:
                        act.wait_ge(*prj["dve"].at("v4", it))
                    else:
                        act.wait_ge(v_loaded, 16 * 6 * (it + 1))
                    act.wait_ge(vpad, 2 if mla else 4)
                    for src, dst in v_parts:
                        act.activation(dst[0], src, ACT.Copy).then_inc(L["stagev"]["act"].sem, 1)

                def stage(it):
                    inc = stg["act"].sem
                    for name, out, n, o, g in (("tq", qT, T, 0, g_q), ("tp", kT, KEYS, 0, g_k),
                                               ("tc", kT, KEYS, SEQ, g_k)):
                        for hh in range(2):
                            act.wait_ge(*stg["pe"].at(f"{name}{hh}", it))
                            kw = {} if g is None else {"scale": g[0:D, :]}
                            act.activation(out[0][0:D, hh * n + o:hh * n + o + SEQ],
                                           ps[0:D, banks[f"{name}{hh}"], :], ACT.Copy, **kw).then_inc(inc, 1)
                    act.wait_ge(*stg["pe"].at("ts", it))
                    for n, (out, g) in enumerate(((qT, g_q), (kT, g_k))):
                        w = T if n == 0 else KEYS
                        kw = {} if g is None else {"scale": g[0:D, :]}
                        act.activation(out[0][0:D, :].rearrange("p (g w) -> p g w", g=2)[:, :, w - DEC:w],
                                       ps[0:D, banks["ts"], n * 2 * DEC:(n + 1) * 2 * DEC
                                          ].rearrange("p (g w) -> p g w", g=2), ACT.Copy, **kw).then_inc(inc, 1)

                def split_units(it):
                    split_hi(0, U + 2 * it, U // 2 + it + 1, QC * 2 * DA)
                    split_hi(1, U + 2 * it + 1, U // 2 + it + 1, LC * 4 * DV)

                def turn_of(p, stages, projects):
                    split_p(0, 0, p)
                    if not mla:
                        stage_values(p)
                    elif stages:
                        square_keys(p + 1)
                    for j in range(1, 4):
                        split_p(0, j, p)
                        exp(1, j - 1, p)
                    exp(1, 3, p)
                    exp(1, 4, p)
                    if stages:
                        stage(p + 1)
                        if mla and projects:
                            split_units(p + 2)
                        elif mla:
                            ahead(U + 2 * PAIRS)
                    split_p(1, 0, p)
                    for j in range(1, 4):
                        split_p(1, j, p)
                        if stages:
                            exp(0, j - 1, p + 1)
                    if stages:
                        exp(0, 3, p + 1)
                        exp(0, 4, p + 1)
                    act.wait_ge(*att["pe"].at("pv1", p))
                    if stages and mla:
                        stage_values(p + 1)
                    act.activation(hid[0][:, bass.ds(p * T, SEQ)], ps[:, 6, :], ACT.Copy).then_inc(att["act"].sem, 1)
                    for hh in range(2):
                        r = slice(hh * DV, (hh + 1) * DV)
                        act.activation(hid[0][r, bass.ds(p * T + SEQ, DEC)], ps[r, 7, hh * DEC:(hh + 1) * DEC],
                                       ACT.Copy).then_inc(att["act"].sem, 1)
                    if mla and projects:
                        project(p + 2)

                if mla:
                    act.wait_ge(stored, 64)
                    split_hi(1, U + 1, U // 2 + 1, LC * 4 * DV)
                    project(0)
                    square_keys(0)
                stage(0)
                if mla:
                    stage_values(0)
                for u in range(5):
                    exp(0, u, 0)
                if mla:
                    split_units(1)
                    project(1)
                with act.Fori(0, PAIRS - 2) as p:
                    turn_of(p, True, True)
                turn_of(PAIRS - 2, True, False)
                turn_of(PAIRS - 1, False, False)

            attention(M, True, gq, gk)
            out_proj(MO)
            ffn_all(F1)

            def square_chunk(st, src):
                act.wait_ge(*st["dve"].at("c4"))
                act.activation(arena[:, 0:NT * 512].rearrange("p (t w) -> p t w", t=NT), src, ACT.Square
                               ).then_inc(st["act"].sem, 1)

            def square_queries(c):
                st, src = Q["k"][c], qn[:, :, 8 * c:8 * c + 8, :].rearrange("p t g w -> p t (g w)")
                act.wait_ge(*st["dve"].at("c4"))
                if c == 1:
                    act.wait_ge(*Q["k"][0]["dve"].at("ss4"))
                act.activation(scr[:, 0:4 * 512].rearrange("p (t w) -> p t w", t=4), src[:, 0:4], ACT.Square
                               ).then_inc(st["act"].sem, 1)
                act.activation(rstd[:, 0:512], src[:, 4], ACT.Square).then_inc(st["act"].sem, 1)

            fg = KV["forget"]
            finc = fg["act"].sem
            f = [stat[:, ST_F:ST_F + 80], scr[:, 0:80], scr[:, 80:160], scr[:, 160:240]]
            for m in range(16):
                ahead(KV["u"] + m + 1)
                if m == 0:
                    root(KV["rms"], KV["x"])
                    act.wait_ge(loaded["fox"], 96)
                    act.activation(mask_causal[:, :], mask_raw[:, :], ACT.Copy).then_inc(finc, 1)
                    act.activation(wfs[0][:, 0:KC * HEADS], wf[:, :], ACT.Copy).then_inc(finc, 1)
                if m == 5:
                    square_chunk(KV["k"][0], chunk[0][:, :, :])
                if m == 7:
                    act.wait_ge(*fg["dve"].at("b"))
                    act.activation(f[1], f[0], ACT.Abs).then_inc(finc, 1)
                    act.wait_ge(*fg["act"].at("abs"))
                    act.activation(f[2], f[1], ACT.Exp, scale=-1.0).then_inc(finc, 1)
                    act.wait_ge(*fg["dve"].at("u"))
                    act.activation(f[1], f[3], ACT.Ln).then_inc(finc, 1)
                if m == 9:
                    square_chunk(KV["k"][1], chunk[1][:, :, :])
            for k in range(KC):
                act.wait_ge(w_used, KV["u"] + 12 + k // 2 + PRIME + 1)
                act.activation(tile(xa[0], k), tile(h, k), ACT.Copy, scale=gc[:, G_FFN + 16 + k:G_FFN + 17 + k]
                               ).then_inc(KV["resplit"]["act"].sem, 1)
            ffn_all(F2)

            for m in range(8):
                ahead(Q["u"] + m + 1)
                if m == 0:
                    root(Q["rms"], Q["x"])
                if m == 5:
                    square_queries(0)
            square_queries(1)
            attention(X, False, gbq, None)
            out_proj(XO)
            ffn_all(F3)
            root(Y["rms"], Y["x"])

        @block.vector
        def _(dve):
            prime(dve, "dve")
            dve.sem_inc(w_lo, PRIME)

            def split_lo(par, u, n):
                dve.wait_ge(w_hi, u + 1)
                dve.tensor_tensor(wl[par][:, 0:n], raw[par][:, 0:n], wh[par][:, 0:n].bitcast(F32), ALU.subtract
                                  ).then_inc(w_lo, 1)

            def ahead(u):
                if u < unit[0]:
                    split_lo(u % 2, u, size[u])

            def low(out, src, hi, scale, inc):
                if scale is None:
                    ins = dve.tensor_tensor(out, src, hi.bitcast(F32), ALU.subtract)
                else:
                    ins = dve.scalar_tensor_tensor(out, src, scale, hi.bitcast(F32), ALU.mult, ALU.subtract)
                ins.then_inc(inc, 1)

            def inverse(rms):
                dve.wait_ge(*rms["act"].at("sd"))
                dve.reciprocal(rstd[:, :], scratch[2]).then_inc(rms["dve"].sem, 1)

            def split_x(k, x, gain):
                dve.wait_ge(*x["act"].at("x_hi", k))
                low(tile(xa[1], k), tile(h, k), tile(xa[0], k), gc[:, bass.ds(gain + k, 1)], x["dve"].sem)

            def ffn_in(q):
                st, U = q["st"], q["u"]
                inc = st["dve"].sem

                def turn(i, n_next, first):
                    split_lo(1, U + 2 * i + 1, KC * P)
                    if first and q["rms"] is not None:
                        inverse(q["rms"])
                        dve.wait_ge(*q["rms"]["dve"].at("r"))
                    dve.wait_ge(w_used, U + 2 * i + PRIME + 1)
                    dve.tensor_tensor(two(scratch[0]), pair(0), two(rstd[:, :]), ALU.mult).then_inc(inc, 1)
                    split_lo(0, U + 2 * i + 2, n_next)
                    dve.wait_ge(w_used, U + 2 * i + 1 + PRIME + 1)
                    dve.tensor_tensor(two(scratch[1]), pair(1), two(rstd[:, :]), ALU.mult).then_inc(inc, 1)
                    dve.wait_ge(*st["act"].at("silu", i))
                    dve.wait_ge(*st["dve"].at("up", i))
                    dve.wait_ge(*st["dve"].at("hid_lo", i - 1))
                    dve.tensor_tensor(scratch[3], scratch[2], scratch[1], ALU.mult).then_inc(inc, 1)
                    dve.wait_ge(*st["act"].at("hid_hi", i))
                    low(tile(hid[1], i), scratch[3], tile(hid[0], i), None, inc)

                turn(0, KC * P, True)
                with dve.Fori(1, FT - 1) as i:
                    turn(i, KC * P, False)
                turn(FT - 1, size[U + 2 * FT], False)

            def out_proj(q):
                st, U, n = q["st"], q["u"], q["kt"] * P

                def turn(i, last):
                    for j in range(2):
                        k = 2 * i + j
                        if last and j == 1:
                            ahead(U + KC)
                        else:
                            split_lo((j + 1) % 2, U + k + 1, n)
                        dve.wait_ge(w_used, U + k + PRIME + 1)
                        dve.scalar_tensor_tensor(two(tile(h, k)), pair(2 + j), q["scale"], two(tile(h, k)),
                                                 ALU.mult, ALU.add).then_inc(st["dve"].sem, 1)
                        if q["what"] == "update":
                            split_x(k, st, q["gain"])

                with dve.Fori(0, KC // 2 - 1) as i:
                    turn(i, False)
                turn(KC // 2 - 1, True)

            def ffn_all(fs):
                for q in fs:
                    ffn_in(q) if q["kind"] == "in" else out_proj(q)

            dve.memset(ones[:, :], 1.0).then_inc(set_dve, 1)
            dve.memset(eps[:, :], EPS).then_inc(set_dve, 1)
            dve.memset(neghalf[:, :], -0.5).then_inc(set_dve, 1)
            dve.memset(gbq[DB:DB + 2, :], 1.0).then_inc(set_dve, 1)
            dve.memset(stat[:, :], 1.0).then_inc(set_dve, 1)
            dve.wait_ge(loaded["gains"], 16)
            for k in range(KC):
                split_x(k, X0, G_FFN)
                if k == 0:
                    ahead(0)
            dve.wait_ge(loaded["const"], 64)
            dve.tensor_scalar(gq[0:DA, :], gq[0:DA, :], float(DA) ** -0.5, None, ALU.mult).then_inc(set_dve, 1)
            dve.tensor_scalar(gbq[0:DB, :], gbq[0:DB, :], float(DB) ** -0.5, None, ALU.mult).then_inc(set_dve, 1)
            ffn_all(F0)

            def rms_tok(step):
                dve.wait_ge(*step["pe"].at("rtok"))
                dve.tensor_copy(rtok[:, :], ps[:, MISC, 0:NT]).then_inc(step["dve"].sem, 1)
                dve.wait_ge(*step["dve"].at("rtok"))

            st, U = Z["st"], Z["u"]
            inc = st["dve"].sem
            for m in range(4):
                ahead(U + m + 1)
                if m == 0:
                    inverse(Z["rms"])
                if m == 1:
                    rms_tok(st)
                if m == 2:
                    for t in range(NT):
                        dve.wait_ge(w_used, U + 1 + PRIME + 1)
                        dve.tensor_scalar(lat[:, t, 0:ZW // 2], ps[:, TOK_BANKS[t], 0:ZW // 2],
                                          rtok[:, t:t + 1], None, ALU.mult).then_inc(inc, 1)
            for t in range(NT):
                dve.wait_ge(w_used, U + 3 + PRIME + 1)
                dve.tensor_scalar(lat[:, t, ZW // 2:ZW], ps[:, TOK_BANKS[(NT + t) % 7], 0:ZW // 2],
                                  rtok[:, t:t + 1], None, ALU.mult).then_inc(inc, 1)
            dve.wait_ge(*st["dve"].at("z14"))
            dve.wait_ge(loaded["mla"], 80)
            kp = lat[:, :, Q_RANK + KV_RANK:ZW]
            hf = ROPE // 2
            ra = scr[:, 2 * T:2 * T + NT * ROPE].rearrange("p (t w) -> p t w", t=NT)
            rb = scr[:, T:T + NT * ROPE].rearrange("p (t w) -> p t w", t=NT)
            dve.tensor_tensor(ra, kp, cos_sin[:, 0], ALU.mult).then_inc(inc, 1)
            dve.tensor_tensor(rb[:, :, 0:hf], kp[:, :, hf:ROPE], cos_sin[:, 1, :, 0:hf], ALU.mult).then_inc(inc, 1)
            dve.tensor_tensor(rb[:, :, hf:ROPE], kp[:, :, 0:hf], cos_sin[:, 1, :, hf:ROPE], ALU.mult
                              ).then_inc(inc, 1)
            dve.wait_ge(*st["dve"].at("rb"))
            dve.tensor_tensor(kpe[:, 0:NT, :], ra, rb, ALU.add).then_inc(inc, 1)
            dve.wait_ge(*st["act"].at("sdk"))
            dve.reciprocal(stat[:, ST_MS + 20:ST_MS + 30], stat[:, ST_MS + 10:ST_MS + 20]).then_inc(inc, 1)
            dve.wait_ge(*st["dve"].at("rstd"))
            for t in range(NT):
                dve.tensor_scalar(lat[:, t, 0:Q_RANK], lat[:, t, 0:Q_RANK],
                                  stat[:, ST_MS + 20 + t:ST_MS + 21 + t], None, ALU.mult).then_inc(inc, 1)
            for t in range(NT):
                c = lat[:, t, Q_RANK:Q_RANK + KV_RANK]
                dve.scalar_tensor_tensor(c, c, stat[:, ST_MS + 25 + t:ST_MS + 26 + t], gkv, ALU.mult, ALU.mult
                                         ).then_inc(inc, 1)
            dve.wait_ge(*st["act"].at("sqpe"))
            dve.reduce_sum(sspe[:, :], scratch[3][:, 0:NK * ROPE].rearrange("p (t w) -> p t w", t=NK), AX.X
                           ).then_inc(inc, 1)
            dve.wait_ge(*st["act"].at("cache"))
            both = [a[:, :].rearrange("p (j w) -> p j w", j=LC)[:, :, SEQ:SEQ + PAST] for a in latT]
            low(both[1], cached_raw.rearrange("p (j w) -> p j w", j=LC), both[0], None, inc)
            for name, n, src in (("t", SEQ, None), ("u", DEC, 5)):
                for j in range(QC + LC):
                    dve.wait_ge(*st["act"].at(f"{name}{j}" if src is None else "u4"))
                    s = ps[:, j, :] if src is None else ps[:, src, j * DEC:(j + 1) * DEC]
                    if j < QC:
                        o = j * T + (0 if src is None else SEQ)
                        low(cqT[1][:, o:o + n], s, cqT[0][:, o:o + n], gc[:, G_AQ + j:G_AQ + j + 1], inc)
                    else:
                        o = (j - QC) * KEYS + (0 if src is None else SEQ + PAST)
                        low(latT[1][:, o:o + n], s, latT[0][:, o:o + n], None, inc)

            def attention(L, mla, g_q, g_k, meanwhile=None):
                att, stg, D, U = L["att"], L["stage"], L["d"], L.get("u")
                prj = L.get("proj")
                ainc = att["dve"].sem
                banks = {n: b for n, b, _, _ in w_uses(L, 0, True, True, True, mla)}

                def top(hh, u, p):
                    r0 = S0 if u == 4 else 0
                    c = ST_NM + 5 * hh + u
                    src = ps[S0:P, 1:3, 0:HALF_T] if u == 4 else ps[:, u % 3, 0:P_W[u]]
                    st = L["head0" if hh == 0 else "att"]
                    dve.wait_ge(*st["pe"].at(f"s{hh}{u}", p))
                    dve.tensor_reduce(stat[r0:P, c:c + 1], src, AX.XY if u == 4 else AX.X, ALU.max, negate=True
                                      ).then_inc(st["dve"].sem, 1)

                def inverse_sums(hh, p):
                    st = L["head0" if hh == 0 else "att"]
                    dve.wait_ge(*st["act"].at(f"exp{hh}4", p))
                    dve.wait_ge(*st["pool"].at(f"d{hh}4", p - 1))
                    dve.reciprocal(stat[:, ST_RI + 5 * hh:ST_RI + 5 * hh + 5], stat[:, ST_RS + 5 * hh:ST_RS + 5 * hh + 5]
                                   ).then_inc(st["dve"].sem, 1)

                def split_p(hh, j, p):
                    o, w = (PT_OFF[j], PT_W[j]) if j < 3 else (PS_OFF[0] if hh == 0 else PT_OFF[3], PT_W[3] + PT_S)
                    dve.wait_ge(*att["act"].at(f"pt{hh}{j}", p))
                    low(pT[1][:, o:o + w], ps[:, banks[f"t{hh}{j}"], 0:w], pT[0][:, o:o + w], None, ainc)

                def take_q(it):
                    for n in range(3):
                        if n == 0:
                            dve.wait_ge(*stg["pe"].at("ts", it - 1))
                        if n < 2:
                            dve.wait_ge(*prj["pe"].at(f"q{n}", it))
                        else:
                            dve.wait_ge(w_used, U + 2 * it + PRIME + 1)
                        w = (2 if n < 2 else 1) * 2 * DA
                        dve.tensor_copy(qs[:, n * 4 * DA:n * 4 * DA + w], ps[:, banks[f"q{n}"], 0:w]
                                        ).then_inc(prj["dve"].sem, 1)

                def project(it):
                    inc = prj["dve"].sem
                    q4 = qs.rearrange("p (t g w) -> p t g w", t=NT, g=2)
                    a = scr[:, 0:NT * 2 * ROPE].rearrange("p (t g w) -> p t g w", t=NT, g=2)
                    b = scr[:, T:T + NT * 2 * ROPE].rearrange("p (t g w) -> p t g w", t=NT, g=2)

                    def table(n, lo, hi):
                        return cos_sin[:, n, :, lo:hi].unsqueeze(2).to_broadcast([P, NT, 2, hi - lo])

                    dve.wait_ge(*prj["dve"].at("q2", it))
                    dve.wait_ge(*prj["dve"].at("ssk", it - 1))
                    dve.tensor_tensor(a, q4[:, :, :, NOPE:DA], table(0, 0, ROPE), ALU.mult).then_inc(inc, 1)
                    dve.tensor_tensor(b[:, :, :, 0:hf], q4[:, :, :, NOPE + hf:DA], table(1, 0, hf), ALU.mult
                                      ).then_inc(inc, 1)
                    dve.tensor_tensor(b[:, :, :, hf:ROPE], q4[:, :, :, NOPE:NOPE + hf], table(1, hf, ROPE), ALU.mult
                                      ).then_inc(inc, 1)
                    dve.wait_ge(*prj["dve"].at("rope_b", it))
                    dve.tensor_tensor(q4[:, :, :, NOPE:DA], a, b, ALU.add).then_inc(inc, 1)
                    for n in range(5):
                        dve.wait_ge(*prj["act"].at(f"k{n}", it))
                        if n == 0:
                            dve.wait_ge(*L["stagev"]["pool"].at("v", it - 1))
                        w = 2 if n < 4 else 1
                        src = ps[:, banks[f"kv{n}"], 0:w * 4 * DV].rearrange("p (t x) -> p t x", t=w)
                        dst = vr.rearrange("p (t x) -> p t x", t=NK)
                        dve.tensor_copy(dst[:, 2 * n:2 * n + w, :], src[:, :, 2 * DV:4 * DV]).then_inc(inc, 1)
                        if n == 1:
                            dve.wait_ge(*prj["act"].at("sqq", it))
                            dve.reduce_sum(stat[:, ST_SS:ST_SS + 10],
                                           scr[:, NK * 2 * NOPE:NK * 2 * NOPE + nq].rearrange("p (t w) -> p t w", w=DA),
                                           AX.X).then_inc(inc, 1)
                            dve.wait_ge(*prj["dve"].at("ssq", it))
                            dve.tensor_scalar(stat[:, ST_VAR:ST_VAR + 10], stat[:, ST_SS:ST_SS + 10], 1.0 / DA, EPS,
                                              ALU.mult, ALU.add).then_inc(inc, 1)

                def mean_square_keys(it):
                    inc = prj["dve"].sem
                    dve.wait_ge(*prj["act"].at("sqk", it))
                    dve.reduce_sum(stat[:, ST_SS + 10:ST_SS + 28],
                                   scr[:, 0:NK * 2 * NOPE].rearrange("p (t w) -> p t w", w=NOPE), AX.X
                                   ).then_inc(inc, 1)
                    dve.wait_ge(*prj["dve"].at("ssk", it))
                    sk = stat[:, ST_SS + 10:ST_SS + 28].rearrange("p (t g) -> p t g", g=2)
                    dve.tensor_tensor(sk, sk, sspe[:, :].unsqueeze(2).to_broadcast([P, NK, 2]), ALU.add
                                      ).then_inc(inc, 1)
                    dve.wait_ge(*prj["dve"].at("ssk2", it))
                    dve.tensor_scalar(stat[:, ST_VAR + 10:ST_VAR + 28], stat[:, ST_SS + 10:ST_SS + 28], 1.0 / DA, EPS,
                                      ALU.mult, ALU.add).then_inc(inc, 1)

                def norm_keys(it):
                    dve.wait_ge(*prj["pool"].at("pow", it))
                    k3 = ks.rearrange("p (t w) -> p t w", w=DA)[:, :, 0:NOPE]
                    rk = stat[:, ST_R + 10:ST_R + 28].unsqueeze(2).to_broadcast([P, 2 * NK, NOPE])
                    dve.tensor_tensor(k3, k3, rk, ALU.mult).then_inc(prj["dve"].sem, 1)

                def stage(it):
                    inc = stg["dve"].sem
                    for name, step, out, n, o, g in (("tq", "q", qT, T, 0, g_q), ("tp", "p", kT, KEYS, 0, g_k),
                                                     ("tc", "c", kT, KEYS, SEQ, g_k)):
                        for hh in range(2):
                            dve.wait_ge(*stg["act"].at(f"{step}{hh}", it))
                            c = slice(hh * n + o, hh * n + o + SEQ)
                            low(out[1][0:D, c], ps[0:D, banks[f"{name}{hh}"], :], out[0][0:D, c],
                                None if g is None else g[0:D, :], inc)
                    for n, (out, g, w) in enumerate(((qT, g_q, T), (kT, g_k, KEYS))):
                        dve.wait_ge(*stg["act"].at("sk", it))
                        o = [x[0:D, :].rearrange("p (g w) -> p g w", g=2)[:, :, w - DEC:w] for x in out]
                        low(o[1], ps[0:D, banks["ts"], n * 2 * DEC:(n + 1) * 2 * DEC
                                     ].rearrange("p (g w) -> p g w", g=2), o[0],
                            None if g is None else g[0:D, :], inc)

                def split_units(it):
                    split_lo(0, U + 2 * it, QC * 2 * DA)
                    split_lo(1, U + 2 * it + 1, LC * 4 * DV)

                def turn_of(p, stages, projects):
                    for j in range(4):
                        top(1, j, p)
                        split_p(0, j, p)
                        if j == 0 and mla and stages:
                            mean_square_keys(p + 1)
                    top(1, 4, p)
                    inverse_sums(1, p)
                    if stages:
                        if mla:
                            norm_keys(p + 1)
                        stage(p + 1)
                        if mla and projects:
                            split_units(p + 2)
                        elif mla:
                            ahead(U + 2 * PAIRS)
                    for j in range(4):
                        if stages:
                            top(0, j, p + 1)
                        split_p(1, j, p)
                    if stages:
                        top(0, 4, p + 1)
                        inverse_sums(0, p + 1)
                    dve.wait_ge(*att["act"].at("o", p))
                    c = bass.ds(p * T, SEQ)
                    low(hid[1][:, c], ps[:, 6, :], hid[0][:, c], None, ainc)
                    for hh in range(2):
                        r, c = slice(hh * DV, (hh + 1) * DV), bass.ds(p * T + SEQ, DEC)
                        dve.wait_ge(*att["act"].at(f"os{hh}", p))
                        low(hid[1][r, c], ps[r, 7, hh * DEC:(hh + 1) * DEC], hid[0][r, c], None, ainc)
                    if mla and projects:
                        take_q(p + 2)
                        project(p + 2)

                if mla:
                    dve.wait_ge(stored, 64)
                    split_lo(1, U + 1, LC * 4 * DV)
                    take_q(0)
                    project(0)
                    mean_square_keys(0)
                    norm_keys(0)
                stage(0)
                for u in range(5):
                    top(0, u, 0)
                inverse_sums(0, 0)
                if meanwhile is not None:
                    meanwhile()
                if mla:
                    split_units(1)
                    take_q(1)
                    project(1)
                with dve.Fori(0, PAIRS - 2) as p:
                    turn_of(p, True, True)
                turn_of(PAIRS - 2, True, False)
                turn_of(PAIRS - 1, False, False)

            attention(M, True, gq, gk)
            out_proj(MO)
            ffn_all(F1)

            def take_chunk(st, last_unit, c, dst, free=None):
                if free is not None:
                    dve.wait_ge(*free)
                dve.wait_ge(w_used, last_unit + PRIME + 1)
                for t in range(NT):
                    dve.tensor_scalar(dst[:, t, :], ps[:, TOK_BANKS[(NT * c + t) % 7], :], rtok[:, t:t + 1], None,
                                      ALU.mult).then_inc(st["dve"].sem, 1)

            def mean_squares(st, n_w):
                inc = st["dve"].sem
                dve.wait_ge(*st["act"].at("sq"))
                dve.reduce_sum(stat[:, ST_SS:ST_SS + 40],
                               arena[:, 0:NT * 512].rearrange("p (t w) -> p t w", w=DB), AX.X).then_inc(inc, 1)
                dve.wait_ge(*st["dve"].at("ss"))
                dve.tensor_scalar(stat[:, ST_VAR:ST_VAR + 40], stat[:, ST_SS:ST_SS + 40], 1.0 / DB, EPS, ALU.mult,
                                  ALU.add).then_inc(inc, 1)

            def mean_square_queries(c):
                st = Q["k"][c]
                inc = st["dve"].sem
                for name, src, o, n in (("sq", scr[:, 0:4 * 512], 0, 32), ("sq4", rstd[:, 0:512], 32, 8)):
                    dve.wait_ge(*st["act"].at(name))
                    dve.reduce_sum(stat[:, ST_SS + o:ST_SS + o + n], src.rearrange("p (t w) -> p t w", w=DB), AX.X
                                   ).then_inc(inc, 1)
                dve.wait_ge(*st["dve"].at("ss4"))
                dve.tensor_scalar(stat[:, ST_VAR:ST_VAR + 40], stat[:, ST_SS:ST_SS + 40], 1.0 / DB, EPS, ALU.mult,
                                  ALU.add).then_inc(inc, 1)

            def normalise(st, x):
                dve.wait_ge(*st["pool"].at("pow"))
                dve.tensor_tensor(x, x, stat[:, ST_R:ST_R + 40].rearrange("p (t g) -> p t g", t=NT).unsqueeze(3)
                                  .to_broadcast([P, NT, 8, DB]), ALU.mult).then_inc(st["dve"].sem, 1)

            def heads(c):
                return chunk[c][:, :, :].rearrange("p t (g w) -> p t g w", g=8)

            fg, U = KV["forget"], KV["u"]
            finc = fg["dve"].sem
            f = [stat[:, ST_F:ST_F + 80], scr[:, 0:80], scr[:, 80:160], scr[:, 160:240], scr[:, 240:320],
                 scr[:, 320:400], scr[:, 400:480]]

            def after(name, eng="dve"):
                dve.wait_ge(*fg[eng].at(name))

            for m in range(16):
                ahead(U + m + 1)
                if m == 0:
                    inverse(KV["rms"])
                    after("whi", "act")
                    for a in wfs:
                        dve.memset(a[:, KC * HEADS:WF].bitcast(F32), 0.0).then_inc(set_dve, 1)
                    low(wfs[1][:, 0:KC * HEADS], wf[:, :], wfs[0][:, 0:KC * HEADS], None, finc)
                if m == 2:
                    rms_tok(KV["rtok"])
                if m == 3:
                    after("f", "pe")
                    for n in range(2):
                        c = slice(n * HALF_T, (n + 1) * HALF_T)
                        dve.tensor_tensor(fT[:, c], ps[0:HEADS, F_BANKS[n], 0:HALF_T], rstd[0:HEADS, c], ALU.mult
                                          ).then_inc(finc, 1)
                if m == 4:
                    take_chunk(KV["k"][0], U + 3, 0, chunk[0])
                    after("ft", "pe")
                    dve.tensor_tensor(f[0].rearrange("p (t w) -> p t w", t=NT),
                                      ps[:, MISC, 16:96].rearrange("p (t w) -> p t w", t=NT),
                                      bf[:, :].unsqueeze(1).to_broadcast([P, NT, HEADS]), ALU.add).then_inc(finc, 1)
                if m == 5:
                    mean_squares(KV["k"][0], DB)
                if m == 6:
                    normalise(KV["k"][0], heads(0))
                if m == 7:
                    after("b")
                    dve.tensor_scalar(f[4], f[0], 0.0, None, ALU.min).then_inc(finc, 1)
                    after("e", "act")
                    dve.tensor_scalar(f[3], f[2], 1.0, None, ALU.add).then_inc(finc, 1)
                    after("u")
                    dve.tensor_scalar(f[5], f[3], -1.0, None, ALU.add).then_inc(finc, 1)
                    after("w")
                    dve.tensor_scalar(f[6], f[5], 0.0, None, ALU.is_equal).then_inc(finc, 1)
                    after("ln", "act")
                    after("z")
                    dve.tensor_tensor(f[1], f[1], f[6], ALU.add).then_inc(finc, 1)
                    dve.tensor_tensor(f[5], f[5], f[6], ALU.add).then_inc(finc, 1)
                    after("wz")
                    dve.reciprocal(f[3], f[5]).then_inc(finc, 1)
                    after("rb")
                    dve.tensor_tensor(f[2], f[2], f[3], ALU.mult).then_inc(finc, 1)
                    after("eb")
                    dve.tensor_tensor(f[1], f[1], f[2], ALU.mult).then_inc(finc, 1)
                    after("l")
                    dve.tensor_tensor(lf[:, 0:NT, :].rearrange("p t w -> p (t w)"), f[4], f[1], ALU.subtract
                                      ).then_inc(finc, 1)
                if m == 8:
                    take_chunk(KV["k"][1], U + 7, 1, chunk[1])
                if m == 9:
                    mean_squares(KV["k"][1], DB)
                if m == 10:
                    normalise(KV["k"][1], heads(1))
                    after("c", "pe")
                    o = ps[:, MISC, 128:128 + NK * HEADS].rearrange("p (t w) -> p t w", t=NK)
                    dve.tensor_copy(cs[:, :, :], o).then_inc(finc, 1)
                    dve.tensor_scalar(ncs[:, :, :], o, -1.0, None, ALU.mult).then_inc(finc, 1)
                if m == 12:
                    take_chunk(KV["v"][0], U + 11, 2, chunk[0], (stored_kv[0], 32))
            take_chunk(KV["v"][1], U + 15, 3, chunk[1], (stored_kv[1], 32))
            for k in range(KC):
                split_x(k, KV["resplit"], G_FFN + 16)
            ffn_all(F2)

            U = Q["u"]
            qv = [qn[:, :, 8 * c:8 * c + 8, :] for c in range(2)]
            for m in range(8):
                ahead(U + m + 1)
                if m == 0:
                    inverse(Q["rms"])
                if m == 2:
                    rms_tok(Q["rtok"])
                if m == 4:
                    for s in range(2):
                        dve.wait_ge(stored_kv[s], 64)
                    take_chunk(Q["k"][0], U + 3, 0, qv[0].rearrange("p t g w -> p t (g w)"))
                if m == 5:
                    mean_square_queries(0)
                if m == 6:
                    normalise(Q["k"][0], qv[0])
            take_chunk(Q["k"][1], U + 7, 1, qv[1].rearrange("p t g w -> p t (g w)"))
            attention(X, False, gbq, None, lambda: mean_square_queries(1))
            out_proj(XO)
            ffn_all(F3)
            inverse(Y["rms"])
            dve.wait_ge(*Y["rms"]["dve"].at("r"))
            for k in range(KC):
                dve.scalar_tensor_tensor(xf[k], tile(h, k), gc[:, G_FIN + k:G_FIN + k + 1], rstd[:, :], ALU.mult,
                                         ALU.mult).then_inc(Y["yout"]["dve"].sem, 1)

        @block.gpsimd
        def _(pool):
            prime(pool, "pool")
            def power(st, n):
                pool.wait_ge(*st["dve"].at("ms"))
                pool.tensor_tensor(stat[:, ST_R:ST_R + n], stat[:, ST_VAR:ST_VAR + n], neghalf[:, 0:n], ALU.pow
                                   ).then_inc(st["pool"].sem, 1)

            def pad():
                for a in vT:
                    pool.memset(a[:, :, DV:2 * DV].bitcast(F32), 0.0).then_inc(vpad, 1)

            def attention(L, mla, meanwhile=None):
                att, stg, D = L["att"], L["stage"], L["d"]
                prj = L.get("proj")
                qsv = qs[:, 0:NT * 2 * D].rearrange("p (t g w) -> p t g w", t=NT, g=2)
                ksv = ks[:, 0:NK * 2 * D].rearrange("p (t g w) -> p t g w", t=NK, g=2)

                def stage_fox(it):
                    inc = L["fstage"]["pool"].sem
                    pool.wait_ge(*stg["pe"].at("ts", it - 1))
                    qf = qn[:, :, :, :].rearrange("p t g w -> p t (g w)")
                    pool.tensor_copy(qsv[:, :, :, 0:DB], qf[:, :, bass.ds(it * 2 * DB, 2 * DB)]
                                     .rearrange("p t (g w) -> p t g w", g=2)).then_inc(inc, 1)
                    for dst, src, n in ((qsv[:, :, :, DB + 1], cs, NT), (ksv[:, :, :, DB], ncs, NK)):
                        pool.tensor_copy(dst, src[:, 0:n, bass.ds(it * 2, 2)]).then_inc(inc, 1)

                def project_at(it):
                    def power(c0, c1):
                        pool.tensor_tensor(stat[:, ST_R + c0:ST_R + c1], stat[:, ST_VAR + c0:ST_VAR + c1],
                                           neghalf[:, 0:c1 - c0], ALU.pow).then_inc(prj["pool"].sem, 1)

                    pool.wait_ge(*prj["dve"].at("msq", it))
                    power(0, 10)
                    pool.wait_ge(*prj["pool"].at("powq", it))
                    q3 = qs.rearrange("p (t w) -> p t w", w=DA)
                    pool.tensor_tensor(q3, q3, stat[:, ST_R:ST_R + 10].unsqueeze(2).to_broadcast([P, 10, DA]),
                                       ALU.mult).then_inc(prj["pool"].sem, 1)
                    pool.wait_ge(*prj["dve"].at("ms", it))
                    power(10, 28)
                    pool.wait_ge(*prj["pool"].at("pow", it))
                    pool.tensor_tensor(ksv[:, :, :, NOPE:DA],
                                       kpe[:, :, :].unsqueeze(2).to_broadcast([P, NK, 2, ROPE]),
                                       stat[:, ST_R + 10:ST_R + 28].rearrange("p (t g) -> p t g", g=2).unsqueeze(3)
                                       .to_broadcast([P, NK, 2, ROPE]), ALU.mult).then_inc(prj["pool"].sem, 1)

                def diagonals(hh, p):
                    st = L["head0" if hh == 0 else "att"]
                    pool.wait_ge(*st["dve"].at(f"r{hh}", p))
                    for u in range(5):
                        pool.wait_ge(*att["pe"].at(f"t{1 - hh}{min(u, 3)}", p - 1 if hh == 0 else p))
                        c = ST_RI + 5 * hh + u
                        pool.tensor_tensor(diag[u], ident[:, :], stat[:, c:c + 1].to_broadcast([P, P]), ALU.mult
                                           ).then_inc(st["pool"].sem, 1)

                def stage_values(it):
                    for step_, (src, dst) in zip(("vp", "v"), v_parts):
                        pool.wait_ge(*L["stagev"]["act"].at(step_, it))
                        pool.tensor_tensor(dst[1], src, dst[0].bitcast(F32), ALU.subtract
                                           ).then_inc(L["stagev"]["pool"].sem, 1)

                def turn_of(p, stages, projects):
                    if not mla:
                        stage_values(p)
                    diagonals(1, p)
                    if stages:
                        diagonals(0, p + 1)
                        if mla:
                            stage_values(p + 1)
                    if projects:
                        step(p + 2)

                step = project_at if mla else stage_fox
                step(0)
                pool.wait_ge(w_used, (Z["u"] + 3 if mla else Q["u"] + 7) + PRIME + 1)
                pad()
                if mla:
                    stage_values(0)
                diagonals(0, 0)
                step(1)
                if meanwhile is not None:
                    meanwhile()
                with pool.Fori(0, PAIRS - 2) as p:
                    turn_of(p, True, True)
                turn_of(PAIRS - 2, True, False)
                turn_of(PAIRS - 1, False, False)

            attention(M, True)
            def store_kv(c):
                if c < 2:
                    pool.wait_ge(*KV["k"][c]["pool"].at("g"))
                else:
                    pool.wait_ge(*KV["v"][c - 2]["dve"].at("c4"))
                o, cols = "o_k" if c < 2 else "o_v", slice((c % 2) * 512, (c % 2) * 512 + 512)
                pool.dma_start(d[o + "_p"].rearrange("(t p) e -> p t e", p=P)[:, :, cols], chunk[c % 2][:, 0:4, :]
                             ).then_inc(stored_kv[c % 2], 16)
                pool.dma_start(d[o + "_s"][:, cols], chunk[c % 2][S0:P, 4, :]).then_inc(stored_kv[c % 2], 16)

            for c in range(2):
                st = KV["k"][c]
                power(st, 40)
                pool.wait_ge(*st["dve"].at("n"))
                x = chunk[c][:, :, :].rearrange("p t (g w) -> p (t g) w", g=8)
                pool.tensor_tensor(x, x, gkn[:, :].unsqueeze(1).to_broadcast([P, 40, DB]), ALU.mult
                                   ).then_inc(st["pool"].sem, 1)
                store_kv(c)
            pool.wait_ge(*KV["forget"]["dve"].at("lf"))
            pool.dma_start(d["o_lf_p"].rearrange("(t p) w -> p t w", p=P), lf[:, 0:4, :]).then_inc(stored_lf, 16)
            pool.dma_start(d["o_lf_s"], lf[S0:P, 4, :]).then_inc(stored_lf, 16)
            for c in range(2, 4):
                store_kv(c)
            pool.wait_ge(*KV["k"][1]["dve"].at("ss"))
            qx = qs[:, 0:NT * 2 * DBX].rearrange("p (t w) -> p t w", w=DBX)
            kx = ks[:, 0:NK * 2 * DBX].rearrange("p (t w) -> p t w", w=DBX)
            pool.memset(qx[:, :, DB:DB + 1], 1.0).then_inc(set_pool, 1)
            pool.memset(kx[:, :, DB + 1:DB + 2], 1.0).then_inc(set_pool, 1)
            power(Q["k"][0], 40)
            pool.wait_ge(*Q["k"][0]["dve"].at("n"))

            def second_queries():
                st = Q["k"][1]
                power(st, 40)
                pool.wait_ge(*st["pool"].at("pow"))
                x = qn[:, :, 8:16, :]
                pool.tensor_tensor(x, x, stat[:, ST_R:ST_R + 40].rearrange("p (t g) -> p t g", t=NT).unsqueeze(3)
                                   .to_broadcast([P, NT, 8, DB]), ALU.mult).then_inc(st["pool"].sem, 1)
                pool.wait_ge(*st["pool"].at("n"))

            attention(X, False, second_queries)


INS = {
    "x": (P, KC * T), "g_cols": (P, 67), "g_a_qk": (2, DA, 1), "g_b_qn": (DB, 1), "g_a_kv": (1, KV_RANK),
    "g_b_kn": (1, DB), "b_b_f": (1, HEADS), "w_ffn_in": (4, HALVES, FT, 2, P, KC * P),
    "w_ffn_out": (4, HALVES, KC, P, FT * P), "w_a_in": (2, 2, P, 4 * ZW // 2), "w_a_qup": (PAIRS, P, QC * 2 * DA),
    "w_a_kvup": (PAIRS, P, LC * 4 * DV), "w_a_out": (KC, P, KC * P), "w_b_kv": (4, 4, P, 1024),
    "w_f": (P, KC * HEADS), "w_b_q": (2, 4, P, 1024), "w_b_out": (KC, P, KC * P), "kpe": (P, 4, ROPE),
    "lat_T": (P, LC * PAST), "fox_k": (PAST, D_MODEL), "fox_v": (PAST, D_MODEL), "logf": (P, 4, HEADS),
    "c_ident": (P, P), "c_mask_chunk": (P, P), "c_mask_causal": (P, P), "c_tri": (P, P),
    "c_rope": (P, 2, NT, ROPE),
}
OUTS = {
    "o_y": (KC, P, T), "o_lat_p": (SEQ, KV_RANK), "o_lat_s": (DEC, KV_RANK), "o_kpe_p": (SEQ, ROPE),
    "o_kpe_s": (DEC, ROPE), "o_k_p": (SEQ, D_MODEL), "o_k_s": (DEC, D_MODEL), "o_v_p": (SEQ, D_MODEL),
    "o_v_s": (DEC, D_MODEL), "o_lf_p": (SEQ, HEADS), "o_lf_s": (DEC, HEADS),
}


def constants():
    i = np.arange(P)
    out = {"c_ident": np.eye(P, dtype=np.float32),
           "c_tri": (i[:, None] <= i[None, :]).astype(np.float32),
           "c_mask_chunk": np.where(i[None, :] // CHUNK <= i[:, None] // CHUNK, 0.0, NEG).astype(np.float32),
           "c_mask_causal": np.where(i[None, :] <= i[:, None], 0.0, NEG).astype(np.float32)}
    half = ROPE // 2
    pos = np.concatenate([np.arange(SEQ), PAST + np.arange(DEC)]).astype(np.float32)
    inv = (np.float32(10000.0) ** (-np.arange(half, dtype=np.float32) / np.float32(half))).astype(np.float32)
    ang = (pos[:, None] * inv[None, :]).astype(np.float32).astype(np.float64)
    cos, sin = np.cos(ang), np.sin(ang)
    table = np.stack([np.concatenate([cos, cos], 1), np.concatenate([-sin, sin], 1)]).astype(np.float32)
    rope = np.stack([table[:, s:s + P] for s in TS])
    out["c_rope"] = np.ascontiguousarray(rope.transpose(2, 1, 0, 3))
    return out


def kernel(**inputs):
    import concourse.bacc as bacc
    from concourse.bass_utils import run_bass_kernel_spmd

    a = {k: np.asarray(v) for k, v in inputs.items()}

    def cols(g):
        g = g.reshape(-1, g.shape[-1])
        return g.reshape(g.shape[0], -1, P).transpose(2, 0, 1).reshape(P, -1)

    x = np.concatenate([a["x_prompt"][0], a["x_sample"][0]], 0).T
    arrays = dict(constants())
    arrays["x"] = x.reshape(KC, P, T).transpose(1, 0, 2).reshape(P, KC * T)
    arrays["g_cols"] = np.concatenate([cols(a["g_ffn"]), cols(a["g_mix"]), cols(a["g_b_kv"]), cols(a["g_final"]),
                                       cols(a["g_a_q"])], 1)
    arrays["g_a_qk"] = a["g_a_qk"].reshape(2, DA, 1)
    arrays["g_b_qn"] = a["g_b_qn"][0].reshape(DB, 1)
    arrays["g_a_kv"] = a["g_a_kv"].reshape(1, KV_RANK)
    arrays["g_b_kn"] = a["g_b_kn"].reshape(1, DB)
    arrays["b_b_f"] = a["b_b_f"].reshape(1, HEADS)
    arrays["w_ffn_in"] = a["w_ffn_in"].reshape(4, KC, P, 2, HALVES, FT, P).transpose(0, 4, 5, 3, 2, 1, 6).reshape(
        INS["w_ffn_in"])
    arrays["w_ffn_out"] = a["w_ffn_out"].reshape(4, HALVES, FT, P, KC, P).transpose(0, 1, 4, 3, 2, 5).reshape(
        INS["w_ffn_out"])
    arrays["w_a_in"] = a["w_a_in"][0].reshape(2, 4, P, 2, ZW // 2).transpose(3, 0, 2, 1, 4).reshape(INS["w_a_in"])
    arrays["w_a_qup"] = a["w_a_qup"][0].reshape(QC, P, PAIRS, 2 * DA).transpose(2, 1, 0, 3).reshape(INS["w_a_qup"])
    arrays["w_a_kvup"] = a["w_a_kvup"][0].reshape(LC, P, PAIRS, 2, 2, DV).transpose(2, 1, 0, 4, 3, 5).reshape(
        INS["w_a_kvup"])
    for n in "ab":
        arrays[f"w_{n}_out"] = a[f"w_{n}_out"][0].reshape(KC, P, KC, P).transpose(2, 1, 0, 3).reshape(
            INS["w_a_out"])
    kvf = a["w_b_kvf"]
    arrays["w_b_kv"] = kvf[:, :2 * D_MODEL].reshape(4, 2, P, 4, 512).transpose(3, 0, 2, 1, 4).reshape(INS["w_b_kv"])
    arrays["w_f"] = kvf[:, 2 * D_MODEL:].reshape(KC, P, HEADS).transpose(1, 0, 2).reshape(INS["w_f"])
    arrays["w_b_q"] = a["w_b_q"][0].reshape(4, 2, P, 2, 512).transpose(3, 0, 2, 1, 4).reshape(INS["w_b_q"])
    arrays["kpe"] = a["cache_mla_kpe"][0, 0].reshape(4, P, ROPE).transpose(1, 0, 2)
    arrays["lat_T"] = a["cache_mla_latent"][0, 0].T.reshape(LC, P, PAST).transpose(1, 0, 2).reshape(INS["lat_T"])
    arrays["fox_k"] = a["cache_fox_k"][0].reshape(PAST, D_MODEL)
    arrays["fox_v"] = a["cache_fox_v"][0].reshape(PAST, D_MODEL)
    arrays["logf"] = a["cache_fox_logf"][0].reshape(4, P, HEADS).transpose(1, 0, 2)
    arrays = {k: np.ascontiguousarray(v) for k, v in arrays.items()}

    nc = bacc.Bacc("TRN2", target_bir_lowering=False, num_devices=1)
    d = {n: nc.dram_tensor(n, s, F32, kind="ExternalInput").ap() for n, s in INS.items()}
    d |= {n: nc.dram_tensor(n, s, F32, kind="ExternalOutput").ap() for n, s in OUTS.items()}
    build(nc, d)
    r = run_bass_kernel_spmd(nc, [arrays], core_ids=[0]).results[0]
    y = r["o_y"].reshape(D_MODEL, T).T
    return (np.ascontiguousarray(y[:SEQ])[None], np.ascontiguousarray(y[SEQ:])[None],
            r["o_lat_p"][None, None], r["o_kpe_p"][None, None],
            r["o_k_p"].reshape(1, SEQ, HEADS, DB), r["o_v_p"].reshape(1, SEQ, HEADS, DB), r["o_lf_p"][None],
            r["o_lat_s"][None, None], r["o_kpe_s"][None, None],
            r["o_k_s"].reshape(1, DEC, HEADS, DB), r["o_v_s"].reshape(1, DEC, HEADS, DB), r["o_lf_s"][None])
```
